# Optimizing a Trainium2 kernel written in Bass

```python
import math
import jax, jax.numpy as jnp
from jax import lax
import numpy as np

D_MODEL = 1024
BATCH = 1
SEQ = 256
DEPTH = 2

N_MIXERS = 2
D_PLE = 256
D_FF = 2816
GLA_HEADS = 4
GLA_DK = D_MODEL // 2 // GLA_HEADS
GLA_DV = D_MODEL // GLA_HEADS
GLA_KEY = GLA_HEADS * GLA_DK
GLA_VAL = GLA_HEADS * GLA_DV
GLA_GATE_RANK = 16
GLA_TAU = 16.0
GLA_CHUNK = 64
GLA_IN = 2 * GLA_KEY + 2 * GLA_VAL + GLA_GATE_RANK
LRU_WIDTH = (D_MODEL * 3) // 2
LRU_BLOCKS = 6
LRU_BLOCK_DIM = LRU_WIDTH // LRU_BLOCKS
LRU_CONV = 4
LRU_C = 8.0
DN_ALPHA = (2.0 * DEPTH) ** 0.25
DN_BETA = (8.0 * DEPTH) ** -0.25
LN_EPS = 1e-5
N_GLA = (DEPTH + 1) // 2
N_LRU = DEPTH // 2

kernel_name = "hybrid_gla_rglru_macaron_deepnorm"

def layer_norm(x, g, b):
    xf = x.astype(jnp.float32)
    mu = jnp.mean(xf, axis=-1, keepdims=True)
    var = jnp.mean(jnp.square(xf - mu), axis=-1, keepdims=True)
    return ((xf - mu) * lax.rsqrt(var + LN_EPS) * g + b).astype(x.dtype)

def swiglu(x, w_in, w_out):
    g, u = jnp.split(x @ w_in, 2, axis=-1)
    return (jax.nn.silu(g) * u) @ w_out

def gla_mixer(x, w_in, w_gate_up, b_gate, norm_g, w_out):
    B, S, _ = x.shape
    C = GLA_CHUNK
    nC = S // C
    proj = x @ w_in
    q, k, v, r, z = jnp.split(
        proj, [GLA_KEY, 2 * GLA_KEY, 2 * GLA_KEY + GLA_VAL, 2 * GLA_KEY + 2 * GLA_VAL], axis=-1)
    log_g = jax.nn.log_sigmoid((z @ w_gate_up + b_gate).astype(jnp.float32)) / GLA_TAU

    def heads(t, d):
        return t.astype(jnp.float32).reshape(B, nC, C, GLA_HEADS, d).transpose(1, 0, 3, 2, 4)

    qc = heads(q, GLA_DK) * (GLA_DK ** -0.5)
    kc = heads(k, GLA_DK)
    vc = heads(v, GLA_DV)
    gc = heads(log_g, GLA_DK)
    causal = jnp.tril(jnp.ones((C, C), dtype=bool))[:, :, None]

    def step(state, inp):
        q_, k_, v_, g_ = inp
        bcum = jnp.cumsum(g_, axis=2)
        o_inter = jnp.einsum('bhtk,bhkv->bhtv', q_ * jnp.exp(bcum), state)
        diff = bcum[:, :, :, None, :] - bcum[:, :, None, :, :]
        decay = jnp.exp(jnp.where(causal, diff, -jnp.inf))
        scores = jnp.einsum('bhtk,bhsk,bhtsk->bhts', q_, k_, decay)
        o = o_inter + jnp.einsum('bhts,bhsv->bhtv', scores, v_)
        b_last = bcum[:, :, -1:, :]
        new_state = (jnp.exp(b_last[:, :, 0, :])[..., None] * state
                     + jnp.einsum('bhsk,bhsv->bhkv', k_ * jnp.exp(b_last - bcum), v_))
        return new_state, o

    state0 = jnp.zeros((B, GLA_HEADS, GLA_DK, GLA_DV), jnp.float32)
    _, o = lax.scan(step, state0, (qc, kc, vc, gc))
    o = o.transpose(1, 0, 3, 2, 4).reshape(B, S, GLA_HEADS, GLA_DV)
    o = o * lax.rsqrt(jnp.mean(jnp.square(o), axis=-1, keepdims=True) + LN_EPS) * norm_g
    o = o.reshape(B, S, GLA_VAL) * jax.nn.silu(r.astype(jnp.float32))
    return (o.astype(x.dtype) @ w_out).astype(x.dtype)

def _lin_comb(c1, c2):
    a1, b1 = c1
    a2, b2 = c2
    return a1 * a2, a2 * b1 + b2

def rglru_mixer(x, w_in, conv_w, conv_b, w_a, b_a, w_i, b_i, lam, w_out):
    B, S, _ = x.shape
    xb, yb = jnp.split(x @ w_in, 2, axis=-1)
    xpad = jnp.pad(xb, ((0, 0), (LRU_CONV - 1, 0), (0, 0)))
    xc = conv_b + sum(xpad[:, j:j + S, :] * conv_w[j] for j in range(LRU_CONV))
    xh = xc.reshape(B, S, LRU_BLOCKS, LRU_BLOCK_DIM)
    r_gate = jax.nn.sigmoid((jnp.einsum('bsnd,nde->bsne', xh, w_a) + b_a).astype(jnp.float32))
    i_gate = jax.nn.sigmoid((jnp.einsum('bsnd,nde->bsne', xh, w_i) + b_i).astype(jnp.float32))
    r_gate = r_gate.reshape(B, S, LRU_WIDTH)
    i_gate = i_gate.reshape(B, S, LRU_WIDTH)
    log_a = -LRU_C * r_gate * jax.nn.softplus(-lam.astype(jnp.float32))
    a = jnp.exp(log_a)
    mult = jnp.sqrt(jnp.maximum(-jnp.expm1(2.0 * log_a), 0.0))
    bx = mult * (i_gate * xc.astype(jnp.float32))
    _, h = lax.associative_scan(_lin_comb, (a, bx), axis=1)
    y = h * jax.nn.gelu(yb.astype(jnp.float32))
    return (y.astype(x.dtype) @ w_out).astype(x.dtype)

def setup_inputs(seed: int = 0) -> dict:
    key = jax.random.key(seed)
    ks = jax.random.split(key, 24)
    f32 = jnp.float32

    def nrm(k, shape, scale):
        return jax.random.normal(k, shape, f32) * scale

    a0 = jax.random.uniform(ks[19], (N_LRU, LRU_WIDTH), f32, 0.9, 0.999) ** (1.0 / LRU_C)
    lru_lambda = jnp.log(a0) - jnp.log1p(-a0)
    return {
        "x": nrm(ks[0], (BATCH, SEQ, D_MODEL), 1.0),
        "p": nrm(ks[1], (DEPTH, BATCH, SEQ, D_PLE), 1.0),
        "ln_g": 1.0 + nrm(ks[2], (DEPTH, 3, D_MODEL), 0.02),
        "ln_b": nrm(ks[3], (DEPTH, 3, D_MODEL), 0.02),
        "ffn_w_in": nrm(ks[4], (DEPTH, 2, D_MODEL, 2 * D_FF), D_MODEL ** -0.5),
        "ffn_w_out": nrm(ks[5], (DEPTH, 2, D_FF, D_MODEL), DN_BETA * D_FF ** -0.5),
        "gla_w_in": nrm(ks[6], (N_GLA, D_MODEL, GLA_IN), D_MODEL ** -0.5),
        "gla_w_gate_up": nrm(ks[7], (N_GLA, GLA_GATE_RANK, GLA_KEY), GLA_GATE_RANK ** -0.5),
        "gla_b_gate": nrm(ks[8], (N_GLA, GLA_KEY), 0.1),
        "gla_norm_g": 1.0 + nrm(ks[9], (N_GLA, GLA_DV), 0.02),
        "gla_w_out": nrm(ks[10], (N_GLA, GLA_VAL, D_MODEL), DN_BETA * GLA_VAL ** -0.5),
        "lru_w_in": nrm(ks[11], (N_LRU, D_MODEL, 2 * LRU_WIDTH), D_MODEL ** -0.5),
        "lru_conv_w": nrm(ks[12], (N_LRU, LRU_CONV, LRU_WIDTH), LRU_CONV ** -0.5),
        "lru_conv_b": nrm(ks[13], (N_LRU, LRU_WIDTH), 0.02),
        "lru_w_a": nrm(ks[14], (N_LRU, LRU_BLOCKS, LRU_BLOCK_DIM, LRU_BLOCK_DIM), LRU_BLOCK_DIM ** -0.5),
        "lru_b_a": nrm(ks[15], (N_LRU, LRU_BLOCKS, LRU_BLOCK_DIM), 0.02),
        "lru_w_i": nrm(ks[16], (N_LRU, LRU_BLOCKS, LRU_BLOCK_DIM, LRU_BLOCK_DIM), LRU_BLOCK_DIM ** -0.5),
        "lru_b_i": nrm(ks[17], (N_LRU, LRU_BLOCKS, LRU_BLOCK_DIM), 0.02),
        "lru_lambda": lru_lambda,
        "lru_w_out": nrm(ks[18], (N_LRU, LRU_WIDTH, D_MODEL), DN_BETA * LRU_WIDTH ** -0.5),
        "ple_w_gate": nrm(ks[20], (DEPTH, D_MODEL, D_MODEL), D_MODEL ** -0.5),
        "ple_b_gate": nrm(ks[21], (DEPTH, D_MODEL), 0.02),
        "ple_w_proj": nrm(ks[22], (DEPTH, D_PLE, D_MODEL), DN_BETA * D_PLE ** -0.5),
    }

def reference(x, p, ln_g, ln_b, ffn_w_in, ffn_w_out, gla_w_in, gla_w_gate_up, gla_b_gate,
              gla_norm_g, gla_w_out, lru_w_in, lru_conv_w, lru_conv_b, lru_w_a, lru_b_a,
              lru_w_i, lru_b_i, lru_lambda, lru_w_out, ple_w_gate, ple_b_gate, ple_w_proj):
    for i in range(DEPTH):
        x = layer_norm(DN_ALPHA * x + 0.5 * swiglu(x, ffn_w_in[i, 0], ffn_w_out[i, 0]),
                       ln_g[i, 0], ln_b[i, 0])
        j = i // N_MIXERS
        if i % N_MIXERS == 0:
            mix = gla_mixer(x, gla_w_in[j], gla_w_gate_up[j], gla_b_gate[j],
                            gla_norm_g[j], gla_w_out[j])
        else:
            mix = rglru_mixer(x, lru_w_in[j], lru_conv_w[j], lru_conv_b[j], lru_w_a[j],
                              lru_b_a[j], lru_w_i[j], lru_b_i[j], lru_lambda[j], lru_w_out[j])
        x = layer_norm(DN_ALPHA * x + mix, ln_g[i, 1], ln_b[i, 1])
        x = layer_norm(DN_ALPHA * x + 0.5 * swiglu(x, ffn_w_in[i, 1], ffn_w_out[i, 1]),
                       ln_g[i, 2], ln_b[i, 2])
        gate = jax.nn.sigmoid(x @ ple_w_gate[i] + ple_b_gate[i])
        x = x + gate * (p[i] @ ple_w_proj[i])
    return x


_drawn_inputs = setup_inputs


def setup_inputs(seed=0):
    import zlib

    import numpy as np

    out = dict(_drawn_inputs(seed))
    spreads = {}
    factors = {'gla_w_gate_up': 2.98,
     'gla_b_gate': 7.034,
     'gla_norm_g': 26.401,
     'lru_conv_b': 3.261,
     'lru_b_a': 64.0,
     'lru_b_i': 56.319,
     'ple_b_gate': 8.0}
    for name, (base, spread) in spreads.items():
        noise = np.random.default_rng([zlib.crc32(name.encode()), seed]).standard_normal(out[name].shape)
        drawn = base * np.exp(spread * noise) if base else spread * noise
        out[name] = __import__('jax').numpy.asarray(drawn.astype(out[name].dtype))
    for name, factor in factors.items():
        out[name] = (out[name] * factor).astype(out[name].dtype)
    return out
```

```python
from contextlib import ExitStack

import numpy as np

import concourse.bass as bass
from concourse import mybir

F32 = mybir.dt.float32
F32R = mybir.dt.float32r
U8 = mybir.dt.uint8
ALU = mybir.AluOpType
ACT = mybir.ActivationFunctionType

P = 128
T = 256
TT = T // P
D = 1024
KD = D // P
HALF = 512
HT = HALF // P
F = 2816
KF = F // P
CHUNKS = F // (HALF // 2)
DP = 256
HEADS = 4
DV = 256
LC = 64
LEVELS = 6
LRU_GROUPS = 3
LT = 4 * LRU_GROUPS
CONV = 4
UNITS = 4
RING = 4
CONV_STEPS = CONV - 1
ALPHA = 4.0 ** 0.25
EPS = 1e-5
TAU = 16.0
LRU_C = 8.0

FFN_IN = 2 * CHUNKS
FFN_OUT = 2 * KF // UNITS
FFN = FFN_IN + FFN_OUT
GLA_OUT = 2 * KD // UNITS
GLA = 1 + 12 + GLA_OUT
LRU_OUT = 2 * LT // UNITS
LRU = 5 * LRU_GROUPS + LRU_OUT
PLE = 5
SIZES = [FFN, GLA, FFN, PLE, FFN, LRU, FFN, PLE]
BASES = [sum(SIZES[:i]) for i in range(len(SIZES))]
PIECES = sum(SIZES)

XT_PARTS = [4, 4, 4, 4, 2, 4, 4, 4]
XT_START = [sum(XT_PARTS[:i]) for i in range(len(XT_PARTS) + 1)]
EPOCH_OF_LN = [1, 2, 3, 5, 6, 7]

C_BGATE = 0
C_NORMG = C_BGATE + HEADS
C_PLEB = C_NORMG + DV
C_CONVW = C_PLEB + 2 * KD
C_CONVB = C_CONVW + LT * CONV
C_BA = C_CONVB + LT
C_BI = C_BA + LT
C_LAM = C_BI + LT
C_IDENT = C_LAM + LT
C_ALL = C_IDENT + P


def build(nc, stream, x_rows_d, xT_d, pT_d, ln_d, params_d, masks_d, out, phases=8):
    ctx = ExitStack()
    with ctx:
        arena_at = nc.sbuf_base
        arena_at += -arena_at % 32
        KB = 1024
        ctx.enter_context(nc.sbuf_tensor("arena", [P, 196 * KB // 4], F32))

        def at(name, kb, shape, dt=F32):
            return nc.alloc_sbuf_tensor_at(name, [P] + shape, dt, offset=arena_at + kb * KB)

        def sb(name, shape, dt=F32):
            return ctx.enter_context(nc.sbuf_tensor(name, [P] + shape, dt))

        def sem(name):
            return ctx.enter_context(nc.semaphore(name))

        x_rows = at("x_rows", 0, [TT, D])
        u_rows = at("u_rows", 8, [TT, D])
        xT_hi = at("xT_hi", 16, [KD, T], F32R)
        xT_lo = at("xT_lo", 24, [KD, T], F32R)
        hT_hi = at("hT_hi", 32, [KF, T], F32R)
        hT_lo = at("hT_lo", 54, [KF, T], F32R)
        silu_t = at("silu_t", 76, [2, HALF])
        hid_t = at("hid_t", 80, [2, HALF])
        raw = at("raw", 84, [RING, UNITS, HALF])
        w_hi = at("w_hi", 116, [RING, UNITS, HALF], F32R)
        w_lo = at("w_lo", 148, [RING, UNITS, HALF], F32R)
        ln_gb = at("ln_gb", 180, [2, D])
        pT = at("p_T", 188, [2, T])
        pT_hi = at("pT_hi", 190, [2, T], F32R)
        pT_lo = at("pT_lo", 192, [2, T], F32R)
        zT_hi = at("zT_hi", 194, [T], F32R)
        zT_lo = at("zT_lo", 195, [T], F32R)
        xT_in = at("xT_in", 8, [KD, T])
        y_T = at("y_T", 8, [KD, T])
        mask_in = at("mask_in", 72, [LEVELS + 1, P])
        sig_T = at("sig_T", 76, [KD, T])
        dec = [at(f"dec{i}", 32 + 4 * i, [HEADS * T]) for i in range(2)]
        v_rows = at("v_rows", 40, [TT, D])
        bcum = at("bcum", 48, [HEADS * T])
        qT = at("qT", 54, [HEADS * T])
        kT = at("kT", 58, [HEADS * T])
        r_rows = at("r_rows", 62, [TT, D])
        scores = at("scores", 70, [2 * HEADS, P])
        qk = [at(f"qk{i}", 76 + 4 * i, [HEADS * T]) for i in range(2)]
        khat_rows = at("khat_rows", 80, [2 * HEADS, P])
        squares = at("squares", 76, [HEADS, DV])
        state = [at(f"state{i}", 16 + 4 * i, [HEADS, DV]) for i in range(3)]
        qhat = at("qhat", 28, [HEADS * T])
        o_rows = at("o_rows", 8, [TT, D])
        gelu_T = at("gelu_T", 44, [4, T])
        xc_T = at("xc_T", 48, [4, T])
        xc_hi = at("xc_hi", 66, [4, T], F32R)
        xc_lo = at("xc_lo", 70, [4, T], F32R)
        r_T = at("r_T", 76, [4, T])
        i_T = at("i_T", 80, [4, T])
        a_T = at("a_T", 8, [4, T])
        m_T = at("m_T", 12, [4, T])

        small_in = sb("small_in", [C_ALL])
        mask = sb("mask", [LEVELS + 1, P], U8)
        lru_c = sb("lru_c", [LT])
        small = sb("small", [6, LT])
        stats = sb("stats", [TT, 2, 6])
        mean_var = sb("mean_var", [TT, 2])
        rstd = sb("rstd", [TT, 2])
        expo = sb("expo", [HEADS])
        o_ms = sb("o_ms", [TT, HEADS])
        o_rstd = sb("o_rstd", [TT, HEADS])
        decay = sb("decay", [HEADS * 4])
        ps = ctx.enter_context(nc.psum_tensor("ps", [P, 8, HALF], F32))
        ident = small_in[:, C_IDENT:C_IDENT + P]

        raw_landed = [sem(f"raw_landed{i}") for i in range(RING)]
        xT_landed, x_landed, params_landed, masks_landed, ln_landed, pT_landed, out_landed = map(
            sem, ["xT_landed", "x_landed", "params_landed", "masks_landed", "ln_landed", "pT_landed", "out_landed"])
        masks_ready = sem("masks_ready")
        hi_ready, lo_ready, piece_used = map(sem, ["hi_ready", "lo_ready", "piece_used"])
        xT_hi_ready, xT_lo_ready = sem("xT_hi_ready"), sem("xT_lo_ready")
        pT_hi_ready, pT_lo_ready = sem("pT_hi_ready"), sem("pT_lo_ready")
        silu_done, hidden_ready, hidden_hi, hidden_lo = map(
            sem, ["silu_done", "hidden_ready", "hidden_hi", "hidden_lo"])
        half_done, tile_done, stats_ready, rstd_ready, x_half_ready, xT_psum = map(
            sem, ["half_done", "tile_done", "stats_ready", "rstd_ready", "x_half_ready", "xT_psum"])
        act_chain, dve_chain, pool_chain = map(sem, ["act_chain", "dve_chain", "pool_chain"])
        (z_psum, z_hi, z_lo, q_psum, q_copied, k_copied, abs_done, softplus_ready, b_ready,
         v_copied, r_silu, r_scaled, d_ready, e_ready, qk_ready, s_psum, s_taken, reset_set,
         khat_ready, khat_psum, khat_copied, qhat_ready, kv_psum, state_ready, o_psum, ms_ready,
         o_rstd_ready, o_ready, oT_psum, oT_hi, oT_lo) = map(sem, [
             "z_psum", "z_hi", "z_lo", "q_psum", "q_copied", "k_copied", "abs_done", "softplus_ready",
             "b_ready", "v_copied", "r_silu", "r_scaled", "d_ready", "e_ready",
             "qk_ready", "s_psum", "s_taken", "reset_set", "khat_ready", "khat_psum", "khat_copied",
             "qhat_ready", "kv_psum", "state_ready", "o_psum", "ms_ready", "o_rstd_ready", "o_ready",
             "oT_psum", "oT_hi", "oT_lo"])
        (lam_exp, c_ready, conv_init, conv_ready, xc_hi_ready, xc_lo_ready, gelu_ready,
         r_ready, i_ready, la_ready, a_ready, th_ready, a2_ready, m2_ready, m_ready, ix_ready,
         h_ready, y_ready, y_hi, y_lo) = map(sem, [
             "lam_exp", "c_ready", "conv_init", "conv_ready", "xc_hi_ready", "xc_lo_ready",
             "gelu_ready", "r_ready", "i_ready", "la_ready", "a_ready", "th_ready", "a2_ready",
             "m2_ready", "m_ready", "ix_ready", "h_ready", "y_ready", "y_hi", "y_lo"])
        (sig_ready, xsum_ready, yT_ready, rows_psum, rows_ready) = map(sem, [
            "sig_ready", "xsum_ready", "yT_ready", "rows_psum", "rows_ready"])

        KINDS = ["ffn", "gla", "ffn", "ple", "ffn", "lru", "ffn", "ple"][:phases]
        n_pieces = BASES[phases] if phases < len(SIZES) else PIECES
        EPOCHS = [0, 1, 2, 3, 4, 5, 6, 7]
        FFN_OF = {0: 0, 2: 1, 4: 2, 6: 3}
        LN_OF = {0: 0, 1: 1, 2: 2, 4: 3, 5: 4, 6: 5}
        PLE_OF = {3: 0, 7: 1}

        def f32(ap):
            return ap.bitcast(F32)

        def tok(t):
            return slice(t * P, (t + 1) * P)

        def half(h):
            return slice(h * HALF, (h + 1) * HALF)

        block = ctx.enter_context(nc.Block())

        @block.sync
        def _(sp):
            sp.dma_start(xT_in[:], xT_d).then_inc(xT_landed, 16)
            for n in range(RING):
                sp.dma_start(raw[:, n].rearrange("p u n -> p (u n)"), stream[n]).then_inc(raw_landed[n], 16)
            full = n_pieces // RING
            with sp.Fori(1, full) as i:
                for s in range(RING):
                    sp.wait_ge(lo_ready, RING * i + (s - RING + 1))
                    sp.dma_start(raw[:, s].rearrange("p u n -> p (u n)"),
                                 stream[bass.ds(RING * i + s, 1), :, :].rearrange("a p n -> p (a n)")
                                 ).then_inc(raw_landed[s], 16)
            for n in range(full * RING, n_pieces):
                sp.wait_ge(lo_ready, n - RING + 1)
                sp.dma_start(raw[:, n % RING].rearrange("p u n -> p (u n)"), stream[n]
                             ).then_inc(raw_landed[n % RING], 16)
            for h in range(2):
                if KINDS[-1] == "ple":
                    sp.wait_ge(rows_ready, 2 * (PLE_OF[phases - 1]) + h + 1)
                else:
                    sp.wait_ge(x_half_ready, 4 * (LN_OF[phases - 1] + 1))
                sp.dma_start(out.rearrange("(t p) d -> p t d", p=P)[:, :, half(h)],
                             x_rows[:, :, half(h)]).then_inc(out_landed, 16)
            sp.wait_ge(out_landed, 32)

        @block.tensor
        def _(pe):
            def piece_ready(n):
                pe.wait_ge(lo_ready, n + 1)

            def epoch_ready(e, tokens):
                parts = XT_PARTS[e]
                pe.wait_ge(xT_lo_ready, XT_START[e] + (parts if tokens else min(2, parts)))

            def feature_units(slot, k0, units, bank, x_hi, x_lo, t0, t1, first, last):
                for u in range(units):
                    k = k0 + u
                    for m in range(HT):
                        o = ps[:, bank + m // 2, (m % 2) * T + t0:(m % 2) * T + t1]
                        wh, wl = (w[:, slot, u, m * P:(m + 1) * P] for w in (w_hi, w_lo))
                        pe.matmul(o, wh, x_hi[:, k, t0:t1], start=first and u == 0 and m % 2 == 0,
                                  stop=False, skip_group_check=True)
                        pe.matmul(o, wh, x_lo[:, k, t0:t1], start=False, stop=False, skip_group_check=True)
                        mm = pe.matmul(o, wl, x_hi[:, k, t0:t1], start=False, stop=last and u == units - 1,
                                       skip_group_check=True)
                return mm

            def row_unit(slot, u, bank, k, t, x_hi, x_lo, first, last):
                o = ps[:, bank, :]
                xh, xl = x_hi[:, k, tok(t)], x_lo[:, k, tok(t)]
                pe.matmul(o, xh, w_hi[:, slot, u, :], start=first, stop=False)
                pe.matmul(o, xh, w_lo[:, slot, u, :], start=False, stop=False)
                return pe.matmul(o, xl, w_hi[:, slot, u, :], start=False, stop=last)

            def feature_chunk(n, bank, x_hi=xT_hi, x_lo=xT_lo):
                for j in range(2):
                    piece_ready(n + j)
                    mm = feature_units((n + j) % RING, UNITS * j, UNITS, bank, x_hi, x_lo, 0, T, j == 0, j == 1)
                    mm.then_inc(piece_used, 1)

            def turn_x(ln, t):
                for h in range(2):
                    pe.wait_ge(x_half_ready, 4 * ln + 2 * t + h + 1)
                    for j in range(HT):
                        mm = pe.transpose(ps[:, 2 * t + h, tok(j)],
                                          x_rows[:, t, h * HALF + j * P:h * HALF + (j + 1) * P], ident)
                    mm.then_inc(xT_psum, 1)

            def first_tokens(e, ln, chunks):
                for t in range(TT):
                    if ln is not None:
                        turn_x(ln, t)
                    epoch_ready(e, t)
                    for n, bank in chunks:
                        for j in range(2):
                            piece_ready(n + j)
                            mm = feature_units((n + j) % RING, UNITS * j, UNITS, bank, xT_hi, xT_lo,
                                               t * P, (t + 1) * P, t == 0 and j == 0, t == 1 and j == 1)
                            if t == 1:
                                mm.then_inc(piece_used, 1)

            def out_proj(ln, n0, K, wait_k):
                units = 2 * K
                late = units - 2 * UNITS
                for q in range(late):
                    h, k = divmod(q, K)
                    n = n0 + q // UNITS
                    if q % UNITS == 0:
                        piece_ready(n)
                    if h == 0:
                        wait_k(k)
                    for t in range(TT):
                        mm = row_unit(n % RING, q % UNITS, 4 + 2 * h + t, k, t, hT_hi, hT_lo, k == 0, k == K - 1)
                    if q % UNITS == UNITS - 1:
                        mm.then_inc(piece_used, 1)
                    elif q == K - 1:
                        mm.then_inc(half_done, 1)
                for t in range(TT):
                    for q in range(late, units):
                        h, k = divmod(q, K)
                        n = n0 + q // UNITS
                        if q % UNITS == 0:
                            piece_ready(n)
                        mm = row_unit(n % RING, q % UNITS, 4 + 2 * h + t, k, t, hT_hi, hT_lo, k == 0, k == K - 1)
                        if t == 1 and q % UNITS == UNITS - 1:
                            mm.then_inc(piece_used, 1)
                    if t == 0:
                        mm.then_inc(tile_done, 1)

            def ffn(i):
                f, n, e = FFN_OF[i], BASES[i], EPOCHS[i]
                ln = None if e in (0, 4) else EPOCH_OF_LN.index(e)
                first_tokens(e, ln, [(n, 0)])
                if e == 4:
                    turn_rows(0)

                with pe.Fori(0, (CHUNKS - 1) // 2) as it:
                    for j in range(2):
                        pe.wait_ge(hidden_ready, 2 * it + (CHUNKS * f + j))
                        for jj in range(2):
                            m = 2 + 2 * j + jj
                            pe.wait_ge(lo_ready, 4 * it + (n + m + 1))
                            mm = feature_units((n + m) % RING, UNITS * jj, UNITS, 2 * ((1 + j) % 2), xT_hi, xT_lo,
                                               0, T, jj == 0, jj == 1)
                            mm.then_inc(piece_used, 1)

                def wait_k(k):
                    if k == 0:
                        pe.wait_ge(hidden_lo, CHUNKS * f + CHUNKS - 1)
                    if k == KF - 2:
                        pe.wait_ge(hidden_lo, CHUNKS * f + CHUNKS)

                out_proj(LN_OF[i], n + FFN_IN, KF, wait_k)

            def ple(i):
                l, n, e = PLE_OF[i], BASES[i], EPOCHS[i]
                first_tokens(e, EPOCH_OF_LN.index(e), [(n, 0)])
                piece_ready(n + 2)
                pe.wait_ge(pT_lo_ready, l + 1)
                for c in range(2):
                    for k in range(2):
                        for m in range(HT):
                            o = ps[:, 2 + 4 * c + m // 2, (m % 2) * T:(m % 2 + 1) * T]
                            wh, wl = (w[:, (n + 2) % RING, 2 * c + k, m * P:(m + 1) * P] for w in (w_hi, w_lo))
                            pe.matmul(o, wh, pT_hi[:, k], start=k == 0 and m % 2 == 0, stop=False,
                                      skip_group_check=True)
                            pe.matmul(o, wh, pT_lo[:, k], start=False, stop=False, skip_group_check=True)
                            mm = pe.matmul(o, wl, pT_hi[:, k], start=False, stop=k == 1, skip_group_check=True)
                mm.then_inc(piece_used, 1)
                feature_chunk(n + 3, 4)
                if l == 1:
                    turn_rows(1)

            def turn_rows(l):
                for h in range(2):
                    pe.wait_ge(yT_ready, 2 * l + h + 1)
                    for t in range(TT):
                        for j in range(HT):
                            mm = pe.transpose(ps[:, 2 + 4 * h + t, tok(j)], y_T[:, HT * h + j, tok(t)], ident)
                    mm.then_inc(rows_psum, 1)
                if l == 0:
                    pe.wait_ge(rows_ready, 2)

            def gla(i):
                n, e, ln = BASES[i], EPOCHS[i], LN_OF[i]
                slot = n % RING
                for t in range(TT):
                    turn_x(EPOCH_OF_LN.index(e), t)
                    epoch_ready(e, t)
                    piece_ready(n)
                    for k in range(KD):
                        o = ps[:, 4, tok(t)]
                        wh, wl = (w[:, slot, k // HT, (k % HT) * P:(k % HT + 1) * P] for w in (w_hi, w_lo))
                        pe.matmul(o, wh, xT_hi[:, k, tok(t)], start=k == 0 and t == 0, stop=False, skip_group_check=True)
                        pe.matmul(o, wh, xT_lo[:, k, tok(t)], start=False, stop=False, skip_group_check=True)
                        mm = pe.matmul(o, wl, xT_hi[:, k, tok(t)], start=False, stop=k == KD - 1, skip_group_check=True)
                    mm.then_inc(z_psum, 1)
                    for j in range(2):
                        piece_ready(n + 1 + j)
                        mm = feature_units((n + 1 + j) % RING, UNITS * j, UNITS, 0, xT_hi, xT_lo,
                                           t * P, (t + 1) * P, t == 0 and j == 0, t == 1 and j == 1)
                mm.then_inc(q_psum, 1)
                pe.wait_ge(z_lo, 1)
                for h in range(HEADS):
                    o = ps[:, 5 + h // 2, (h % 2) * T:(h % 2 + 1) * T]
                    wh, wl = (w[:, slot, 2, h * P:(h + 1) * P] for w in (w_hi, w_lo))
                    pe.matmul(o, wh, zT_hi[:], start=h % 2 == 0, stop=False, skip_group_check=True)
                    pe.matmul(o, wh, zT_lo[:], start=False, stop=False, skip_group_check=True)
                    mm = pe.matmul(o, wl, zT_hi[:], start=False, stop=True, skip_group_check=True)
                mm.then_inc(piece_used, 3)
                feature_chunk(n + 3, 2)

                def rows_piece(m, bank):
                    j = (m - 5) % 2
                    piece_ready(n + m)
                    for u in range(UNITS):
                        for t in range(TT):
                            mm = row_unit((n + m) % RING, u, bank + t, UNITS * j + u, t, xT_hi, xT_lo,
                                          j == 0 and u == 0, j == 1 and u == UNITS - 1)
                    mm.then_inc(piece_used, 1)

                def level(l):
                    bank = 4 + 2 * (l % 2)
                    if l < LEVELS:
                        pe.wait_ge(qk_ready, 2 * (l + 1))
                    if l == 0:
                        pe.wait_ge(b_ready, 1)
                    if l >= 2:
                        pe.wait_ge(s_taken, l - 1)
                    for g in range(2 * HEADS):
                        a, b = (qk[l % 2], qk[l % 2]) if l < LEVELS else (kT, qT)
                        mm = pe.matmul(ps[:, bank + g // 4, (g % 4) * P:(g % 4 + 1) * P], a[:, g * P:(g + 1) * P],
                                       b[:, g * P:(g + 1) * P], start=True, stop=True, skip_group_check=True)
                    mm.then_inc(s_psum, 1)

                pe.wait_ge(q_copied, 1)
                rows_piece(5, 0)
                rows_piece(6, 0)
                level(0)
                pe.wait_ge(k_copied, 1)
                rows_piece(7, 2)
                level(1)
                rows_piece(8, 2)
                level(2)
                pe.wait_ge(v_copied, 1)
                rows_piece(9, 0)
                level(3)
                rows_piece(10, 0)
                level(4)
                pe.wait_ge(v_copied, 2)
                rows_piece(11, 2)
                level(5)
                rows_piece(12, 2)
                level(6)
                pe.wait_ge(khat_ready, 1)
                pe.wait_ge(r_silu, 1)
                for g in range(2 * HEADS):
                    mm = pe.transpose(ps[:, g // 4, (g % 4) * P:(g % 4 + 1) * P], qk[0][:, g * P:(g + 1) * P], ident)
                mm.then_inc(khat_psum, 1)
                pe.wait_ge(khat_copied, 1)
                for c, bank in enumerate([2, 0, 4]):
                    if c == 0:
                        pe.wait_ge(r_silu, 2)
                    if c == 2:
                        pe.wait_ge(s_taken, LEVELS + 1)
                    rows = slice(LC * (c % 2), LC * (c % 2) + LC)
                    for h in range(HEADS):
                        mm = pe.matmul(ps[:, bank + h // 2, (h % 2) * DV:(h % 2 + 1) * DV],
                                       khat_rows[rows, 2 * h + c // 2, :],
                                       v_rows[rows, c // 2, h * DV:(h + 1) * DV],
                                       start=True, stop=True, skip_group_check=True)
                    mm.then_inc(kv_psum, 1)
                pe.wait_ge(s_taken, LEVELS + 1)
                pe.wait_ge(qhat_ready, 1)
                for t, bank in ((0, 6), (1, 2)):
                    pe.wait_ge(state_ready, 1 + 2 * t)
                    for h in range(HEADS):
                        o = ps[:, bank + h // 2, (h % 2) * DV:(h % 2 + 1) * DV]
                        mm = pe.matmul(o, scores[:, 2 * h + t, :], v_rows[:, t, h * DV:(h + 1) * DV],
                                       start=True, stop=False, skip_group_check=True)
                        for c in (2 * t, 2 * t + 1):
                            if c > 0:
                                oc = ps[LC * (c % 2):LC * (c % 2) + LC, bank + h // 2, (h % 2) * DV:(h % 2 + 1) * DV]
                                mm = pe.matmul(oc, qhat[:, h * T + c * LC:h * T + (c + 1) * LC], state[c - 1][:, h, :],
                                               start=False, stop=True, skip_group_check=True)
                    mm.then_inc(o_psum, 1)
                for t, bank in ((0, 4), (1, 0)):
                    pe.wait_ge(o_ready, HEADS * (t + 1))
                    for h in range(2):
                        for j in range(HT):
                            mm = pe.transpose(ps[:, bank + h, tok(j)],
                                              o_rows[:, t, h * HALF + j * P:h * HALF + (j + 1) * P], ident)
                        mm.then_inc(oT_psum, 1)

                def wait_k(k):
                    if k == 0:
                        pe.wait_ge(oT_lo, 4)

                out_proj(ln, n + 13, KD, wait_k)

            def lru(i):
                n, e, ln = BASES[i], EPOCHS[i], LN_OF[i]
                for g in range(LRU_GROUPS):
                    m = n + 5 * g
                    if g == 0:
                        first_tokens(e, EPOCH_OF_LN.index(e), [(m, 0)])
                    else:
                        pe.wait_ge(conv_ready, CONV_STEPS * g)
                        feature_chunk(m, 0)
                    if g:
                        pe.wait_ge(gelu_ready, g)
                    feature_chunk(m + 2, 2)
                    piece_ready(m + 4)
                    pe.wait_ge(xc_lo_ready, g + 1)
                    if g:
                        pe.wait_ge(i_ready, 4 * g)
                    slot = (m + 4) % RING
                    for b in range(2):
                        for gate in range(2):
                            for k in range(2):
                                for mt in range(2):
                                    o = ps[:, 4 + 2 * gate + b, mt * T:(mt + 1) * T]
                                    wh, wl = (w[:, slot, 2 * b + gate, k * T + mt * P:k * T + (mt + 1) * P]
                                              for w in (w_hi, w_lo))
                                    pe.matmul(o, wh, xc_hi[:, 2 * b + k], start=k == 0 and mt == 0, stop=False,
                                              skip_group_check=True)
                                    pe.matmul(o, wh, xc_lo[:, 2 * b + k], start=False, stop=False,
                                              skip_group_check=True)
                                    mm = pe.matmul(o, wl, xc_hi[:, 2 * b + k], start=False, stop=k == 1,
                                                   skip_group_check=True)
                    mm.then_inc(piece_used, 1)

                def wait_k(k):
                    if k == 0:
                        pe.wait_ge(i_ready, LT)
                    if k % 4 == 0:
                        pe.wait_ge(y_lo, k // 4 + 1)

                out_proj(ln, n + 5 * LRU_GROUPS, LT, wait_k)

            pe.wait_ge(params_landed, 16)
            for i, kind in enumerate(KINDS):
                {"ffn": ffn, "gla": gla, "lru": lru, "ple": ple}[kind](i)
            if KINDS[-1] != "ple":
                turn_x(LN_OF[phases - 1], 0)
                turn_x(LN_OF[phases - 1], 1)
            if KINDS[-1] == "ple" and phases == 4:
                turn_rows(0)


        @block.scalar
        def _(act):
            issued = [0]
            links = [0]

            def split_one(slot, landed, free):
                act.wait_ge(raw_landed[slot], landed)
                if free is not None:
                    act.wait_ge(piece_used, free)
                act.activation(w_hi[:, slot], raw[:, slot], ACT.Copy).then_inc(hi_ready, 1)

            def split_to(m):
                while issued[0] <= min(m, n_pieces - 1):
                    n = issued[0]
                    split_one(n % RING, 16 * (n // RING + 1), n - RING + 1 if n >= RING else None)
                    issued[0] += 1

            def chain(ins):
                links[0] += 1
                ins.then_inc(act_chain, 1)
                act.wait_ge(act_chain, links[0])

            def x_parts(ln, t):
                e = EPOCH_OF_LN[ln]
                for h in range(2):
                    act.wait_ge(xT_psum, 4 * ln + 2 * t + h + 1)
                    act.activation(xT_hi[:, HT * h:HT * (h + 1), tok(t)],
                                   ps[:, 2 * t + h, :].rearrange("p (j n) -> p j n", n=P), ACT.Copy
                                   ).then_inc(xT_hi_ready, 1)

            def out_split(ln, n0, K):
                last = n0 + 2 * K // UNITS - 1
                split_to(last + 3)
                x_parts(ln, 0)
                x_parts(ln, 1)

            def ffn(i):
                f, n = FFN_OF[i], BASES[i]

                def chunk(par, before, after, c, silu_free):
                    before()
                    act.wait_ge(piece_used, 2 * c + (n + 2))
                    if silu_free is not None:
                        act.wait_ge(hidden_ready, silu_free)
                    act.activation(silu_t[:, par], ps[:, 2 * par, :], ACT.Silu).then_inc(silu_done, 1)
                    after()
                    act.wait_ge(hidden_ready, c + (CHUNKS * f + 1))
                    act.activation(hT_hi[:, bass.ds(2 * c, 2), :],
                                   hid_t[:, par].rearrange("p (k t) -> p k t", t=T), ACT.Copy).then_inc(hidden_hi, 1)

                if i == 4:
                    rows_back(0)
                split_to(n + 2)
                if f:
                    load_p(f)
                chunk(0, lambda: split_to(n + 3), lambda: split_to(n + 4), 0, None)
                with act.Fori(0, (CHUNKS - 1) // 2) as it:
                    for j in range(2):
                        def split(m):
                            split_one((n + m) % RING, 16 * it + 16 * ((n + m) // RING + 1), 4 * it + (n + m - 3))
                        chunk((1 + j) % 2, lambda: split(5 + 2 * j), lambda: split(6 + 2 * j), 2 * it + (1 + j),
                              2 * it + (CHUNKS * f + j))
                issued[0] += 4 * ((CHUNKS - 1) // 2)
                out_split(LN_OF[i], n + FFN_IN, KF)

            def load_p(f):
                if f in (1, 3):
                    act.wait_ge(pT_landed, 16 * (f // 2 + 1))
                    if f == 3:
                        act.wait_ge(piece_used, BASES[3] + 3)
                    act.activation(pT_hi[:], pT[:], ACT.Copy).then_inc(pT_hi_ready, 1)

            def ple(i):
                l, n = PLE_OF[i], BASES[i]
                split_to(n + 3)
                for c in range(2):
                    act.wait_ge(piece_used, n + 2 + 3 * c)
                    for m in range(HT):
                        act.activation(sig_T[:, HT * c + m], ps[:, 4 * c + m // 2, (m % 2) * T:(m % 2 + 1) * T], ACT.Sigmoid,
                                       bias=small_in[:, C_PLEB + KD * l + HT * c + m:C_PLEB + KD * l + HT * c + m + 1]
                                       ).then_inc(sig_ready, 1)
                    if c == 0:
                        split_to(n + 5)
                if l == 0:
                    for h in range(2):
                        act.wait_ge(yT_ready, 2 * l + h + 1)
                        act.activation(xT_hi[:, HT * h:HT * (h + 1)], y_T[:, HT * h:HT * (h + 1)], ACT.Copy
                                       ).then_inc(xT_hi_ready, 1)
                    split_to(n + 6)
                if l == 1 or phases == 4:
                    rows_back(l)

            def rows_back(l):
                for h in range(2):
                    act.wait_ge(rows_psum, 2 * l + h + 1)
                    act.activation(x_rows[:, :, half(h)], ps[:, 2 + 4 * h:4 + 4 * h, :], ACT.Copy).then_inc(rows_ready, 1)

            def gla(i):
                n, ln = BASES[i], LN_OF[i]
                S = lambda m: split_to(n + m)
                S(2)
                act.wait_ge(z_psum, 2)
                act.activation(zT_hi[:], ps[:, 4, 0:T], ACT.Copy).then_inc(z_hi, 1)
                S(3)
                act.wait_ge(q_psum, 1)
                act.activation(qT[:], ps[:, 0:2, :].rearrange("p a b -> p (a b)"), ACT.Copy,
                               scale=float(P) ** -0.5).then_inc(q_copied, 1)
                S(4)
                act.wait_ge(piece_used, n + 3)
                for h in range(HEADS):
                    act.activation(dec[0][:, h * T:(h + 1) * T], ps[:, 5 + h // 2, (h % 2) * T:(h % 2 + 1) * T], ACT.Abs,
                                   bias=small_in[:, C_BGATE + h:C_BGATE + h + 1]).then_inc(abs_done, 1)
                act.wait_ge(abs_done, HEADS)
                chain(act.activation(dec[0][:], dec[0][:], ACT.Exp, scale=-1.0))
                act.activation(dec[0][:], dec[0][:], ACT.Ln, bias=1.0).then_inc(softplus_ready, 1)
                S(5)
                act.wait_ge(piece_used, n + 5)
                act.activation(kT[:], ps[:, 2:4, :].rearrange("p a b -> p (a b)"), ACT.Copy).then_inc(k_copied, 1)
                S(6)

                def decay_of(l):
                    act.wait_ge(d_ready, 2 * (l + 1))
                    act.activation(dec[l % 2][:], dec[l % 2][:], ACT.Exp, scale=1.0 / TAU).then_inc(e_ready, 1)

                def v_copy(c):
                    act.wait_ge(piece_used, n + 7 + 2 * c)
                    act.activation(v_rows[:, :, half(c)], ps[:, 2 * c:2 * c + 2, :], ACT.Copy).then_inc(v_copied, 1)

                def r_gate(c):
                    act.wait_ge(piece_used, n + 11 + 2 * c)
                    act.activation(r_rows[:, :, half(c)], ps[:, 2 * c:2 * c + 2, :], ACT.Silu).then_inc(r_silu, 1)

                decay_of(0)
                S(7)
                decay_of(1)
                S(8)
                decay_of(2)
                S(9)
                v_copy(0)
                decay_of(3)
                S(10)
                decay_of(4)
                S(11)
                v_copy(1)
                decay_of(5)
                S(12)
                act.wait_ge(qk_ready, 2 * 5)
                act.activation(dec[0][:], bcum[:], ACT.Exp, scale=1.0 / TAU).then_inc(e_ready, 1)
                act.wait_ge(d_ready, 2 * LEVELS + 1)
                act.activation(dec[1][:], dec[1][:], ACT.Exp, scale=1.0 / TAU).then_inc(e_ready, 1)
                S(13)
                r_gate(0)
                S(14)
                r_gate(1)
                S(16)
                act.wait_ge(khat_psum, 1)
                act.wait_ge(s_psum, LEVELS)
                act.activation(khat_rows[:].rearrange("p a b -> p (a b)"), ps[:, 0:2, :].rearrange("p a b -> p (a b)"),
                               ACT.Copy).then_inc(khat_copied, 1)
                act.wait_ge(kv_psum, 1)
                act.activation(state[0][:].rearrange("p a b -> p (a b)"), ps[:, 2:4, :].rearrange("p a b -> p (a b)"),
                               ACT.Copy).then_inc(state_ready, 1)
                for t, bank in ((0, 6), (1, 2)):
                    act.wait_ge(o_psum, t + 1)
                    if t:
                        act.wait_ge(ms_ready, HEADS)
                    for h in range(HEADS):
                        act.activation(squares[:, h], ps[:, bank + h // 2, (h % 2) * DV:(h % 2 + 1) * DV], ACT.Square,
                                       accum_out=o_ms[:, t, h:h + 1]).then_inc(ms_ready, 1)
                for t, bank in ((0, 4), (1, 0)):
                    for h in range(2):
                        act.wait_ge(oT_psum, 2 * t + h + 1)
                        act.activation(hT_hi[:, HT * h:HT * (h + 1), tok(t)],
                                       ps[:, bank + h, :].rearrange("p (j n) -> p j n", n=P), ACT.Copy).then_inc(oT_hi, 1)
                out_split(ln, n + 13, KD)

            def lru(i):
                n, ln = BASES[i], LN_OF[i]
                for g in range(LRU_GROUPS):
                    S = lambda m: split_to(n + 5 * g + m)
                    S(3)
                    act.wait_ge(piece_used, n + 5 * g + 2)
                    if g:
                        act.wait_ge(ix_ready, g)
                    for j in range(4):
                        ch = 4 * g + j
                        w = C_CONVW + ch * CONV + CONV - 1
                        act.activation(xc_T[:, j], ps[:, j // 2, (j % 2) * T:(j % 2 + 1) * T], ACT.Identity,
                                       scale=small_in[:, w:w + 1], bias=small_in[:, C_CONVB + ch:C_CONVB + ch + 1]
                                       ).then_inc(conv_init, 1)
                    S(4)
                    act.wait_ge(conv_ready, CONV_STEPS * (g + 1))
                    if g:
                        act.wait_ge(piece_used, n + 5 * g)
                    act.activation(xc_hi[:], xc_T[:], ACT.Copy).then_inc(xc_hi_ready, 1)
                    S(5)
                    act.wait_ge(piece_used, n + 5 * g + 4)
                    if g:
                        act.wait_ge(y_ready, g)
                    act.activation(gelu_T[:].rearrange("p a b -> p (a b)"), ps[:, 2:4, :].rearrange("p a b -> p (a b)"),
                                   ACT.Gelu_apprx_tanh).then_inc(gelu_ready, 1)
                    S(6)
                    act.wait_ge(piece_used, n + 5 * g + 5)
                    if g:
                        act.wait_ge(y_hi, g)
                        act.wait_ge(y_lo, g)
                    for gate, dst, done, bias in ((0, r_T, r_ready, C_BA), (1, i_T, i_ready, C_BI)):
                        for j in range(4):
                            act.activation(dst[:, j], ps[:, 4 + 2 * gate + j // 2, (j % 2) * T:(j % 2 + 1) * T], ACT.Sigmoid,
                                           bias=small_in[:, bias + 4 * g + j:bias + 4 * g + j + 1]).then_inc(done, 1)
                    S(7)
                    act.wait_ge(la_ready, 4 * (g + 1))
                    act.activation(a_T[:], r_T[:], ACT.Exp).then_inc(a_ready, 1)
                    act.activation(m_T[:], r_T[:], ACT.Tanh).then_inc(th_ready, 1)
                    act.wait_ge(a_ready, g + 1)
                    act.wait_ge(th_ready, g + 1)
                    act.activation(r_T[:], a_T[:], ACT.Square).then_inc(a2_ready, 1)
                    act.wait_ge(m2_ready, g + 1)
                    act.activation(m_T[:], m_T[:], ACT.Sqrt).then_inc(m_ready, 1)
                    S(8)
                    act.wait_ge(y_ready, g + 1)
                    act.activation(hT_hi[:, 4 * g:4 * (g + 1)], i_T[:], ACT.Copy).then_inc(y_hi, 1)
                out_split(ln, n + 5 * LRU_GROUPS, LT)

            act.wait_ge(params_landed, 16)
            chain(act.activation(small[:, 0], small_in[:, C_LAM:C_LAM + LT], ACT.Abs))
            act.activation(small[:, 0], small[:, 0], ACT.Exp, scale=-1.0).then_inc(lam_exp, 1)
            act.wait_ge(xT_landed, 16)
            for t in range(TT):
                for h in range(2):
                    act.activation(xT_hi[:, HT * h:HT * (h + 1), tok(t)], xT_in[:, HT * h:HT * (h + 1), tok(t)], ACT.Copy
                                   ).then_inc(xT_hi_ready, 1)
            for i, kind in enumerate(KINDS):
                {"ffn": ffn, "gla": gla, "lru": lru, "ple": ple}[kind](i)

        @block.vector
        def _(dve):
            issued = [0]
            links = [0]

            def split_one(slot, ready):
                dve.wait_ge(hi_ready, ready)
                dve.tensor_tensor(w_lo[:, slot], raw[:, slot], f32(w_hi[:, slot]), ALU.subtract).then_inc(lo_ready, 1)

            def split_to(m):
                while issued[0] <= min(m, n_pieces - 1):
                    split_one(issued[0] % RING, issued[0] + 1)
                    issued[0] += 1

            def chain(ins):
                links[0] += 1
                ins.then_inc(dve_chain, 1)
                dve.wait_ge(dve_chain, links[0])

            def add_residual(t, h, coef):
                chain(dve.scalar_tensor_tensor(out=u_rows[:, t, half(h)], in0=ps[:, 4 + 2 * h + t, :], scalar=coef,
                                               in1=x_rows[:, t, half(h)], op0=ALU.mult, op1=ALU.add))
                chain(dve.bn_stats(stats[:, t, h], u_rows[:, t, half(h)]))

            def x_low(ln, t):
                e = EPOCH_OF_LN[ln]
                for h in range(2):
                    dve.wait_ge(xT_hi_ready, XT_START[e] + 2 * t + h + 1)
                    dst = (slice(None), slice(HT * h, HT * (h + 1)), tok(t))
                    dve.tensor_tensor(xT_lo[dst], ps[:, 2 * t + h, :].rearrange("p (j n) -> p j n", n=P),
                                      f32(xT_hi[dst]), ALU.subtract).then_inc(xT_lo_ready, 1)

            def out_norm(ln, n0, K, coef):
                last = n0 + 2 * K // UNITS - 1
                split_to(n0 + (K - 1) // UNITS + 3)
                if K % UNITS:
                    dve.wait_ge(half_done, ln // 3 * 2 + (ln % 3) // 2 + 1)
                else:
                    dve.wait_ge(piece_used, n0 + K // UNITS)
                for t in range(TT):
                    add_residual(t, 0, coef)
                split_to(last + 2)
                dve.wait_ge(ln_landed, 16 * (ln + 1))
                for t in range(TT):
                    if t == 0:
                        dve.wait_ge(tile_done, ln + 1)
                    else:
                        dve.wait_ge(piece_used, last + 1)
                    add_residual(t, 1, coef)
                    dve.bn_aggr(mean_var[:, t], stats[:, t].rearrange("p a b -> p (a b)")).then_inc(stats_ready, 1)
                    if t == 1:
                        x_low(ln, 0)
                        split_to(last + 3)
                    dve.wait_ge(stats_ready, 2 * ln + t + 1)
                    chain(dve.scalar_tensor_tensor(out=u_rows[:, t], in0=u_rows[:, t], scalar=mean_var[:, t, 0:1],
                                                   in1=ln_gb[:, 0], op0=ALU.subtract, op1=ALU.mult))
                    dve.wait_ge(rstd_ready, 2 * ln + t + 1)
                    for h in range(2):
                        dve.scalar_tensor_tensor(out=x_rows[:, t, half(h)], in0=u_rows[:, t, half(h)],
                                                 scalar=rstd[:, t, 1:2], in1=ln_gb[:, 1, half(h)],
                                                 op0=ALU.mult, op1=ALU.add).then_inc(x_half_ready, 1)
                x_low(ln, 1)

            def ffn(i):
                f, n = FFN_OF[i], BASES[i]

                def chunk(par, before, after, c, hid_free):
                    before()
                    dve.wait_ge(silu_done, c + (CHUNKS * f + 1))
                    if hid_free is not None:
                        dve.wait_ge(hidden_hi, hid_free)
                    dve.tensor_tensor(hid_t[:, par], silu_t[:, par], ps[:, 2 * par + 1, :], ALU.mult
                                      ).then_inc(hidden_ready, 1)
                    after()
                    dve.wait_ge(hidden_hi, c + (CHUNKS * f + 1))
                    dst = hT_lo[:, bass.ds(2 * c, 2), :]
                    dve.tensor_tensor(dst, hid_t[:, par].rearrange("p (k t) -> p k t", t=T),
                                      f32(hT_hi[:, bass.ds(2 * c, 2), :]), ALU.subtract).then_inc(hidden_lo, 1)

                split_to(n + 2)
                if f in (1, 3):
                    dve.wait_ge(pT_hi_ready, f // 2 + 1)
                    dve.tensor_tensor(pT_lo[:], pT[:], f32(pT_hi[:]), ALU.subtract).then_inc(pT_lo_ready, 1)
                chunk(0, lambda: split_to(n + 3), lambda: split_to(n + 4), 0, None)
                with dve.Fori(0, (CHUNKS - 1) // 2) as it:
                    for j in range(2):
                        def split(m):
                            split_one((n + m) % RING, 4 * it + (n + m + 1))
                        chunk((1 + j) % 2, lambda: split(5 + 2 * j), lambda: split(6 + 2 * j), 2 * it + (1 + j),
                              2 * it + (CHUNKS * f + j))
                issued[0] += 4 * ((CHUNKS - 1) // 2)
                if i == 0:
                    dve.wait_ge(x_landed, 16)
                if i == 4:
                    dve.wait_ge(rows_ready, 2)
                out_norm(LN_OF[i], n + FFN_IN, KF, 0.5 / ALPHA)

            def ple(i):
                l, n, e = PLE_OF[i], BASES[i], EPOCHS[i] + 1
                split_to(n + 3)
                dve.wait_ge(xsum_ready, l + 1)
                dve.wait_ge(piece_used, n + 3)
                for c in range(2):
                    dve.wait_ge(sig_ready, KD * l + HT * (c + 1))
                    part = (slice(None), slice(HT * c, HT * (c + 1)))
                    chain(dve.tensor_tensor(sig_T[part].rearrange("p a b -> p (a b)"), sig_T[part].rearrange("p a b -> p (a b)"),
                                            ps[:, 2 + 4 * c:4 + 4 * c, :].rearrange("p a b -> p (a b)"), ALU.mult))
                    dve.tensor_tensor(y_T[part], y_T[part], sig_T[part], ALU.add).then_inc(yT_ready, 1)
                    if c == 0:
                        split_to(n + 5)
                if l == 0:
                    for h in range(2):
                        dve.wait_ge(xT_hi_ready, XT_START[e] + h + 1)
                        part = (slice(None), slice(HT * h, HT * (h + 1)))
                        dve.tensor_tensor(xT_lo[part], y_T[part], f32(xT_hi[part]), ALU.subtract).then_inc(xT_lo_ready, 1)
                    split_to(n + 6)

            def gla(i):
                n, ln = BASES[i], LN_OF[i]
                S = lambda m: split_to(n + m)
                S(2)
                dve.wait_ge(z_hi, 1)
                dve.tensor_tensor(zT_lo[:], ps[:, 4, 0:T], f32(zT_hi[:]), ALU.subtract).then_inc(z_lo, 1)
                S(3)
                dve.wait_ge(abs_done, HEADS)
                for h in range(HEADS):
                    last = dve.tensor_scalar(dec[1][:, h * T:(h + 1) * T], ps[:, 5 + h // 2, (h % 2) * T:(h % 2 + 1) * T],
                                             small_in[:, C_BGATE + h:C_BGATE + h + 1], 0.0, ALU.add, ALU.min)
                    if h < HEADS - 1:
                        last.then_inc(dve_chain, 1)
                links[0] += HEADS - 1
                chain(last)
                S(4)
                dve.wait_ge(softplus_ready, 1)
                chain(dve.tensor_tensor(dec[1][:], dec[1][:], dec[0][:], ALU.subtract))
                dve.wait_ge(reset_set, 2)
                dve.tensor_tensor_scan(bcum[:], qk[0][:], dec[1][:], 0.0, ALU.mult, ALU.add).then_inc(b_ready, 1)
                S(6)

                def operands(l):
                    size = LC >> l
                    dve.wait_ge(e_ready, l + 1)
                    if l == 0:
                        dve.wait_ge(q_copied, 1)
                        dve.wait_ge(k_copied, 1)
                        dve.wait_ge(b_ready, 1)
                    if l >= 2:
                        dve.wait_ge(s_psum, l - 1)
                    for src, part in ((kT, slice(0, size // 2)), (qT, slice(size // 2, size))):
                        blocks = [a[:].rearrange("p (b s) -> p b s", s=size)[:, :, part] for a in (qk[l % 2], dec[l % 2], src)]
                        dve.tensor_tensor(*blocks, ALU.mult).then_inc(qk_ready, 1)

                def take(l):
                    dve.wait_ge(s_psum, l + 1)
                    bank = 4 + 2 * (l % 2)
                    dve.copy_predicated(scores[:], mask[:, l:l + 1, :].to_broadcast([P, 2 * HEADS, P]),
                                        ps[:, bank:bank + 2, :].rearrange("p a (b n) -> p (a b) n", n=P)
                                        ).then_inc(s_taken, 1)
                    dve.wait_ge(s_taken, l + 1)

                operands(0)
                S(7)
                for l in range(LEVELS + 1):
                    if l + 1 < LEVELS:
                        operands(l + 1)
                    if l == LEVELS - 1:
                        dve.wait_ge(e_ready, LEVELS + 2)
                        dve.wait_ge(s_psum, LEVELS - 1)
                        dve.tensor_tensor(qk[0][:], dec[1][:], kT[:], ALU.mult).then_inc(khat_ready, 1)
                        dve.tensor_copy(decay[:], dec[0][:].rearrange("p (b s) -> p b s", s=LC)[:, :, LC - 1]
                                        ).then_inc(dve_chain, 1)
                        links[0] += 1
                    S(8 + l)
                    if l == 0:
                        dve.wait_ge(reset_set, 3)
                        dve.wait_ge(masks_ready, 1)
                    take(l)
                dve.wait_ge(piece_used, n + 13)
                dve.tensor_tensor(qhat[:], dec[0][:], qT[:], ALU.mult).then_inc(qhat_ready, 1)
                S(16)
                dve.wait_ge(dve_chain, links[0])
                dve.wait_ge(state_ready, 1)
                for c in (1, 2):
                    bank = 4 * (c - 1)
                    dve.wait_ge(kv_psum, c + 1)
                    for h in range(HEADS):
                        ins = dve.scalar_tensor_tensor(out=state[c][:, h], in0=state[c - 1][:, h],
                                                       scalar=decay[:, h * 4 + c:h * 4 + c + 1],
                                                       in1=ps[:, bank + h // 2, (h % 2) * DV:(h % 2 + 1) * DV],
                                                       op0=ALU.mult, op1=ALU.add)
                        if h < HEADS - 1:
                            chain(ins)
                    ins.then_inc(state_ready, 1)
                    dve.wait_ge(state_ready, c + 1)
                dve.wait_ge(r_scaled, 1)
                for t, bank in ((0, 6), (1, 2)):
                    dve.wait_ge(o_rstd_ready, t + 1)
                    for h in range(HEADS):
                        dve.scalar_tensor_tensor(out=o_rows[:, t, h * DV:(h + 1) * DV],
                                                 in0=ps[:, bank + h // 2, (h % 2) * DV:(h % 2 + 1) * DV],
                                                 scalar=o_rstd[:, t, h:h + 1], in1=r_rows[:, t, h * DV:(h + 1) * DV],
                                                 op0=ALU.mult, op1=ALU.mult).then_inc(o_ready, 1)
                for t, bank in ((0, 4), (1, 0)):
                    for h in range(2):
                        dve.wait_ge(oT_hi, 2 * t + h + 1)
                        dst = (slice(None), slice(HT * h, HT * (h + 1)), tok(t))
                        dve.tensor_tensor(hT_lo[dst], ps[:, bank + h, :].rearrange("p (j n) -> p j n", n=P),
                                          f32(hT_hi[dst]), ALU.subtract).then_inc(oT_lo, 1)
                out_norm(ln, n + 13, KD, 1.0 / ALPHA)

            def lru(i):
                n, ln = BASES[i], LN_OF[i]
                for g in range(LRU_GROUPS):
                    S = lambda m: split_to(n + 5 * g + m)
                    S(3)
                    dve.wait_ge(conv_init, 4 * (g + 1))
                    for back in range(1, CONV):
                        for j in range(4):
                            w = C_CONVW + (4 * g + j) * CONV + CONV - 1 - back
                            ins = dve.scalar_tensor_tensor(out=xc_T[:, j, back:], in0=ps[:, j // 2, (j % 2) * T:(j % 2 + 1) * T - back],
                                                           scalar=small_in[:, w:w + 1], in1=xc_T[:, j, back:],
                                                           op0=ALU.mult, op1=ALU.add)
                            if j < 3:
                                chain(ins)
                        ins.then_inc(conv_ready, 1)
                        dve.wait_ge(conv_ready, CONV_STEPS * g + back)
                    S(4)
                    dve.wait_ge(xc_hi_ready, g + 1)
                    dve.tensor_tensor(xc_lo[:], xc_T[:], f32(xc_hi[:]), ALU.subtract).then_inc(xc_lo_ready, 1)
                    S(7)
                    dve.wait_ge(r_ready, 4 * (g + 1))
                    if g == 0:
                        dve.wait_ge(c_ready, 1)
                    for j in range(4):
                        dve.tensor_scalar(r_T[:, j], r_T[:, j], lru_c[:, 4 * g + j:4 * g + j + 1], None, ALU.mult
                                          ).then_inc(la_ready, 1)
                    dve.wait_ge(i_ready, 4 * (g + 1))
                    chain(dve.tensor_tensor(i_T[:], i_T[:], xc_T[:], ALU.mult))
                    dve.wait_ge(a2_ready, g + 1)
                    chain(dve.scalar_tensor_tensor(out=m_T[:], in0=r_T[:], scalar=1.0, in1=m_T[:], op0=ALU.add, op1=ALU.mult))
                    dve.tensor_scalar(m_T[:], m_T[:], -1.0, 0.0, ALU.mult, ALU.max).then_inc(m2_ready, 1)
                    S(8)
                    dve.wait_ge(m_ready, g + 1)
                    dve.tensor_tensor(i_T[:], i_T[:], m_T[:], ALU.mult).then_inc(ix_ready, 1)
                    dve.wait_ge(ix_ready, g + 1)
                    for j in range(4):
                        dve.tensor_tensor_scan(r_T[:, j], a_T[:, j], i_T[:, j], 0.0, ALU.mult, ALU.add).then_inc(h_ready, 1)
                    dve.wait_ge(h_ready, 4 * (g + 1))
                    dve.wait_ge(gelu_ready, g + 1)
                    dve.tensor_tensor(i_T[:], r_T[:], gelu_T[:], ALU.mult).then_inc(y_ready, 1)
                    dve.wait_ge(y_hi, g + 1)
                    dve.tensor_tensor(hT_lo[:, 4 * g:4 * (g + 1)], i_T[:], f32(hT_hi[:, 4 * g:4 * (g + 1)]), ALU.subtract
                                      ).then_inc(y_lo, 1)
                out_norm(ln, n + 5 * LRU_GROUPS, LT, 1.0 / ALPHA)

            for t in range(TT):
                for h in range(2):
                    dve.wait_ge(xT_hi_ready, 2 * t + h + 1)
                    part = (slice(None), slice(HT * h, HT * (h + 1)), tok(t))
                    dve.tensor_tensor(xT_lo[part], xT_in[part], f32(xT_hi[part]), ALU.subtract).then_inc(xT_lo_ready, 1)
            split_to(2)
            u, s, s2, poly, neg = (small[:, j] for j in range(5))
            dve.wait_ge(lam_exp, 1)
            chain(dve.tensor_scalar(s, u, 2.0, None, ALU.add))
            chain(dve.reciprocal(s, s))
            chain(dve.tensor_tensor(s, s, u, ALU.mult))
            chain(dve.tensor_tensor(s2, s, s, ALU.mult))
            chain(dve.tensor_scalar(poly, s2, 1.0 / 19, 1.0 / 17, ALU.mult, ALU.add))
            for odd in range(15, 0, -2):
                chain(dve.tensor_tensor(poly, poly, s2, ALU.mult))
                chain(dve.tensor_scalar(poly, poly, 1.0 / odd, None, ALU.add))
            chain(dve.tensor_tensor(poly, poly, s, ALU.mult))
            chain(dve.tensor_scalar(neg, small_in[:, C_LAM:C_LAM + LT], -1.0, 0.0, ALU.mult, ALU.max))
            chain(dve.scalar_tensor_tensor(out=poly, in0=poly, scalar=2.0, in1=neg, op0=ALU.mult, op1=ALU.add))
            dve.tensor_scalar(lru_c[:], poly, -LRU_C, None, ALU.mult).then_inc(c_ready, 1)
            dve.wait_ge(masks_landed, 16)
            dve.tensor_copy(mask[:], mask_in[:]).then_inc(masks_ready, 1)
            for i, kind in enumerate(KINDS):
                {"ffn": ffn, "gla": gla, "lru": lru, "ple": ple}[kind](i)

        @block.gpsimd
        def _(pool):
            links = [0]

            def chain(ins):
                links[0] += 1
                ins.then_inc(pool_chain, 1)
                pool.wait_ge(pool_chain, links[0])

            def load_ln(ln):
                if ln < 6:
                    if ln:
                        pool.wait_ge(x_half_ready, 4 * ln)
                    pool.dma_start(ln_gb[:].rearrange("p a b -> p (a b)"), ln_d[ln].partition_broadcast(P)
                                   ).then_inc(ln_landed, 16)

            def inverse_root(dst, src, scale, eps):
                width = dst.shape[-1]
                chain(pool.tensor_scalar(dst, src, scale, eps, ALU.mult, ALU.add))
                return pool.tensor_tensor(dst, dst, expo[:, 0:width], ALU.pow)

            def norm(ln):
                for t in range(TT):
                    pool.wait_ge(stats_ready, 2 * ln + t + 1)
                    inverse_root(rstd[:, t, 1:2], mean_var[:, t, 1:2], 1.0, EPS / ALPHA ** 2).then_inc(rstd_ready, 1)
                load_ln(ln + 1)

            def gla(i):
                pool.wait_ge(piece_used, BASES[1])
                pool.memset(qk[0][:], 1.0).then_inc(reset_set, 1)
                pool.wait_ge(reset_set, 1)
                pool.memset(qk[0][:].rearrange("p (b s) -> p b s", s=LC)[:, :, 0:1], 0.0).then_inc(reset_set, 1)
                pool.memset(scores[:], 0.0).then_inc(reset_set, 1)
                pool.wait_ge(b_ready, 1)
                for l in range(LEVELS):
                    size = LC >> l
                    bb = bcum[:].rearrange("p (b s) -> p b s", s=size)
                    dd = dec[l % 2][:].rearrange("p (b s) -> p b s", s=size)
                    mid = bb[:, :, size // 2 - 1:size // 2].to_broadcast([P, HEADS * T // size, size // 2])
                    if l >= 2:
                        pool.wait_ge(qk_ready, 2 * (l - 1))
                    pool.tensor_tensor(dd[:, :, 0:size // 2], mid, bb[:, :, 0:size // 2], ALU.subtract).then_inc(d_ready, 1)
                    pool.tensor_tensor(dd[:, :, size // 2:size], bb[:, :, size // 2:size], mid, ALU.subtract
                                       ).then_inc(d_ready, 1)
                bb = bcum[:].rearrange("p (b s) -> p b s", s=LC)
                pool.wait_ge(qk_ready, 2 * LEVELS)
                pool.tensor_tensor(dec[1][:].rearrange("p (b s) -> p b s", s=LC),
                                   bb[:, :, LC - 1:LC].to_broadcast([P, HEADS * T // LC, LC]), bb, ALU.subtract
                                   ).then_inc(d_ready, 1)
                pool.wait_ge(r_silu, 2)
                rr = r_rows[:].rearrange("p t (h v) -> p (t h) v", v=DV)
                pool.tensor_tensor(rr, rr, small_in[:, C_NORMG:C_NORMG + DV].unsqueeze(1).to_broadcast([P, TT * HEADS, DV]),
                                   ALU.mult).then_inc(r_scaled, 1)
                for t in range(TT):
                    pool.wait_ge(ms_ready, HEADS * (t + 1))
                    inverse_root(o_rstd[:, t], o_ms[:, t], 1.0 / DV, EPS).then_inc(o_rstd_ready, 1)
                norm(LN_OF[i])

            def ple(i):
                l, e = PLE_OF[i], EPOCHS[i]
                pool.wait_ge(xT_lo_ready, XT_START[e + 1] if e + 1 < len(XT_START) else 0)
                pool.tensor_tensor(y_T[:], f32(xT_hi[:]), f32(xT_lo[:]), ALU.add).then_inc(xsum_ready, 1)
                if l == 0:
                    pool.wait_ge(pT_lo_ready, 1)
                    pool.dma_start(pT[:], pT_d[1]).then_inc(pT_landed, 16)

            pool.dma_start(small_in[:], params_d).then_inc(params_landed, 16)
            pool.dma_start(mask_in[:], masks_d).then_inc(masks_landed, 16)
            pool.dma_start(x_rows[:], x_rows_d).then_inc(x_landed, 16)
            pool.dma_start(pT[:], pT_d[0]).then_inc(pT_landed, 16)
            load_ln(0)
            chain(pool.memset(expo[:], -0.5))
            for i, kind in enumerate(KINDS):
                if kind in ("ffn", "lru"):
                    norm(LN_OF[i])
                else:
                    {"gla": gla, "ple": ple}[kind](i)


def level_masks():
    s, t = np.meshgrid(np.arange(P), np.arange(P), indexing="ij")
    out = []
    for l in range(LEVELS):
        size = LC >> l
        out.append((s // size == t // size) & (s % size < size // 2) & (t % size >= size // 2))
    out.append(s == t)
    return np.stack(out, 1).astype(np.float32)


def pack(x, p, ln_g, ln_b, ffn_w_in, ffn_w_out, gla_w_in, gla_w_gate_up, gla_b_gate, gla_norm_g, gla_w_out,
         lru_w_in, lru_conv_w, lru_conv_b, lru_w_a, lru_b_a, lru_w_i, lru_b_i, lru_lambda, lru_w_out,
         ple_w_gate, ple_b_gate, ple_w_proj):
    zero = np.zeros((P, HALF), np.float32)

    def chunks(w):
        return [w[k * P:(k + 1) * P, c * HALF:(c + 1) * HALF]
                for c in range(w.shape[1] // HALF) for k in range(w.shape[0] // P)]

    def ffn(layer, which):
        w = ffn_w_in[layer, which]
        q = HALF // 2
        paired = np.concatenate([w[:, o + q * c:o + q * (c + 1)] for c in range(CHUNKS) for o in (0, F)], 1)
        return chunks(paired) + chunks(ffn_w_out[layer, which])

    def gla():
        w = gla_w_in[0]
        kw = HEADS * P
        cuts = [0, kw, 2 * kw, 2 * kw + D, 2 * kw + 2 * D]
        wz = w[:, cuts[4]:]
        z = np.zeros((KD, P, P), np.float32)
        z[:, :, :wz.shape[1]] = wz.reshape(KD, P, -1)
        z = z.transpose(1, 0, 2).reshape(P, KD * P)
        up = zero.copy()
        up[:wz.shape[1]] = gla_w_gate_up[0]
        parts = [w[:, a:b] for a, b in zip(cuts, cuts[1:])]
        return [z[:, :HALF], z[:, HALF:], up, zero] + sum(map(chunks, parts), []) + chunks(gla_w_out[0])

    def lru():
        w = lru_w_in[0]
        width = w.shape[1] // 2
        units = []
        for g in range(LRU_GROUPS):
            cols = slice(g * HALF, (g + 1) * HALF)
            units += chunks(w[:, :width][:, cols]) + chunks(w[:, width:][:, cols])
            for b in (2 * g, 2 * g + 1):
                for m in (lru_w_a, lru_w_i):
                    units.append(np.concatenate([m[0, b, :P], m[0, b, P:]], 1))
        return units + chunks(lru_w_out[0])

    def ple(layer):
        gate, proj = chunks(ple_w_gate[layer]), chunks(ple_w_proj[layer])
        return gate[:KD] + proj + gate[KD:]

    units = ffn(0, 0) + gla() + ffn(0, 1) + ple(0) + ffn(1, 0) + lru() + ffn(1, 1) + ple(1)
    stream = np.empty((PIECES, P, UNITS, HALF), np.float32)
    for q, unit in enumerate(units):
        stream[q // UNITS, :, q % UNITS] = unit
    assert len(units) == PIECES * UNITS

    def column(v):
        return np.asarray(v).reshape(-1, P).T

    small = np.concatenate([
        column(gla_b_gate[0]), np.broadcast_to(gla_norm_g[0], (P, DV)), column(ple_b_gate),
        lru_conv_w[0].T.reshape(LT, P, CONV).transpose(1, 0, 2).reshape(P, LT * CONV), column(lru_conv_b[0]),
        column(lru_b_a[0]), column(lru_b_i[0]), column(lru_lambda[0]), np.eye(P, dtype=np.float32)], 1)
    return {
        "stream": stream.reshape(PIECES, P, UNITS * HALF),
        "x_rows": x[0].reshape(TT, P, D).transpose(1, 0, 2),
        "xT": x[0].T.reshape(KD, P, T).transpose(1, 0, 2),
        "pT": p[:, 0].transpose(0, 2, 1).reshape(2, 2, P, T).transpose(0, 2, 1, 3),
        "ln": np.stack([ln_g, ln_b], 2).reshape(6, 2 * D),
        "params": small,
        "masks": level_masks(),
    }


def kernel(**inputs):
    import concourse.bacc as bacc
    from concourse.bass_utils import run_bass_kernel_spmd

    arrays = {k: np.ascontiguousarray(v) for k, v in pack(**{k: np.asarray(v) for k, v in inputs.items()}).items()}
    nc = bacc.Bacc("TRN2", target_bir_lowering=False, num_devices=1)
    args = [nc.dram_tensor(k, v.shape, mybir.dt.from_np(v.dtype), kind="ExternalInput").ap() for k, v in arrays.items()]
    out = nc.dram_tensor("out", [T, D], F32, kind="ExternalOutput").ap()
    build(nc, *args, out)
    r = run_bass_kernel_spmd(nc, [arrays], core_ids=[0])
    return r.results[0]["out"].reshape(1, T, D)
```

```python
from contextlib import ExitStack

import numpy as np

import concourse.bass as bass
from concourse import mybir

F32 = mybir.dt.float32
F32R = mybir.dt.float32r
U8 = mybir.dt.uint8
ALU = mybir.AluOpType
ACT = mybir.ActivationFunctionType

P = 128
T = 256
TT = T // P
D = 1024
KD = D // P
HALF = 512
HT = HALF // P
F = 2816
KF = F // P
CHUNKS = F // (HALF // 2)
DP = 256
HEADS = 4
DV = 256
LC = 64
LEVELS = 6
LRU_GROUPS = 3
LT = 4 * LRU_GROUPS
CONV = 4
UNITS = 4
RING = 4
CONV_STEPS = (CONV - 1) * HT
ALPHA = 4.0 ** 0.25
EPS = 1e-5
TAU = 16.0
LRU_C = 8.0

FFN_IN = 2 * CHUNKS
FFN_OUT = 2 * KF // UNITS
FFN = FFN_IN + FFN_OUT
GLA_OUT = 2 * KD // UNITS
GLA = 1 + 12 + GLA_OUT
LRU_OUT = 2 * LT // UNITS
LRU = 5 * LRU_GROUPS + LRU_OUT
CONV_AT = [0, 4, 9]
GELU_AT = [2, 7, 12]
GATES_AT = [6, 11, 14]
PLE = 5
SIZES = [FFN, GLA, FFN, PLE, FFN, LRU, FFN, PLE]
BASES = [sum(SIZES[:i]) for i in range(len(SIZES))]
PIECES = sum(SIZES)

C_BGATE = 0
C_NORMG = C_BGATE + HEADS
C_CONVW = C_NORMG + DV
C_CONVB = C_CONVW + LT * CONV
C_BA = C_CONVB + LT
C_BI = C_BA + LT
C_LAM = C_BI + LT
C_IDENT = C_LAM + LT
C_ALL = C_IDENT + P


def build(nc, stream, x_rows_d, xT_d, pT_d, row_params_d, params_d, masks_d, out, phases=8):
    ctx = ExitStack()
    with ctx:
        arena_at = nc.sbuf_base
        arena_at += -arena_at % 32
        KB = 1024
        ctx.enter_context(nc.sbuf_tensor("arena", [P, 196 * KB // 4], F32))

        def at(name, kb, shape, dt=F32):
            return nc.alloc_sbuf_tensor_at(name, [P] + shape, dt, offset=arena_at + kb * KB)

        def sb(name, shape, dt=F32):
            return ctx.enter_context(nc.sbuf_tensor(name, [P] + shape, dt))

        def sem(name):
            return ctx.enter_context(nc.semaphore(name))

        x_rows = at("x_rows", 0, [TT, D])
        u_rows = at("u_rows", 8, [TT, D])
        xT_hi = at("xT_hi", 16, [KD, T], F32R)
        xT_lo = at("xT_lo", 24, [KD, T], F32R)
        hT_hi = at("hT_hi", 32, [KF, T], F32R)
        hT_lo = at("hT_lo", 54, [KF, T], F32R)
        silu_t = at("silu_t", 76, [2, HALF])
        hid_t = at("hid_t", 80, [2, HALF])
        raw = at("raw", 84, [RING, UNITS, HALF])
        w_hi = at("w_hi", 116, [RING, UNITS, HALF], F32R)
        w_lo = at("w_lo", 148, [RING, UNITS, HALF], F32R)
        row_params = at("row_params", 180, [2, D])
        pT = at("p_T", 188, [2, T])
        pT_hi = at("pT_hi", 190, [2, T], F32R)
        pT_lo = at("pT_lo", 192, [2, T], F32R)
        zT_hi = at("zT_hi", 194, [T], F32R)
        zT_lo = at("zT_lo", 195, [T], F32R)
        xT_in = at("xT_in", 8, [KD, T])
        first_rows = at("first_rows", 76, [TT, HALF])
        ple_gate = at("ple_gate", 32, [2, TT, HALF])
        mask_in = at("mask_in", 190, [LEVELS + 1, P])
        dec = [at(f"dec{i}", 32 + 4 * i, [HEADS * T]) for i in range(2)]
        v_rows = at("v_rows", 40, [TT, D])
        bcum = at("bcum", 48, [HEADS * T])
        qT = at("qT", 54, [HEADS * T])
        kT = at("kT", 58, [HEADS * T])
        r_rows = at("r_rows", 62, [TT, D])
        scores = at("scores", 70, [2 * HEADS, P])
        qk = [at(f"qk{i}", 76 + 4 * i, [HEADS * T]) for i in range(2)]
        khat_rows = at("khat_rows", 80, [2 * HEADS, P])
        squares = at("squares", 76, [HEADS, DV])
        state = [at(f"state{i}", 16 + 4 * i, [HEADS, DV]) for i in range(3)]
        qhat = at("qhat", 28, [HEADS * T])
        o_rows = at("o_rows", 8, [TT, D])
        gelu_T = at("gelu_T", 44, [4, T])
        xc_T = [at("xc_T0", 48, [4, T]), at("xc_T1", 190, [4, T])]
        xc_hi = at("xc_hi", 66, [4, T], F32R)
        xc_lo = at("xc_lo", 70, [4, T], F32R)
        r_T = [at("r_T0", 76, [4, T]), at("r_T1", 40, [4, T])]
        i_T = [at("i_T0", 80, [4, T]), at("i_T1", 62, [4, T])]
        a_T = at("a_T", 8, [4, T])
        m_T = at("m_T", 12, [4, T])

        small_in = sb("small_in", [C_ALL])
        mask = sb("mask", [LEVELS + 1, P], U8)
        lru_c = sb("lru_c", [LT])
        small = sb("small", [6, LT])
        stats = sb("stats", [TT, 2, 6])
        mean_var = sb("mean_var", [TT, 2])
        rstd = sb("rstd", [TT, 2])
        expo = sb("expo", [HEADS])
        o_ms = sb("o_ms", [TT, HEADS])
        o_rstd = sb("o_rstd", [TT, HEADS])
        decay = sb("decay", [HEADS * 4])
        ps = ctx.enter_context(nc.psum_tensor("ps", [P, 8, HALF], F32))
        ident = small_in[:, C_IDENT:C_IDENT + P]

        raw_landed = [sem(f"raw_landed{i}") for i in range(RING)]
        x_landed, params_landed, masks_landed, row_params_landed, pT_landed, out_landed = map(
            sem, ["x_landed", "params_landed", "masks_landed", "row_params_landed", "pT_landed", "out_landed"])
        masks_ready = sem("masks_ready")
        hi_ready, lo_ready, piece_used = map(sem, ["hi_ready", "lo_ready", "piece_used"])
        xT_hi_ready, xT_lo_ready = sem("xT_hi_ready"), sem("xT_lo_ready")
        pT_hi_ready, pT_lo_ready = sem("pT_hi_ready"), sem("pT_lo_ready")
        silu_done, hidden_ready, hidden_hi, hidden_lo = map(
            sem, ["silu_done", "hidden_ready", "hidden_hi", "hidden_lo"])
        half_done, tile_done, stats_ready, rstd_ready, x_half_ready, xT_psum = map(
            sem, ["half_done", "tile_done", "stats_ready", "rstd_ready", "x_half_ready", "xT_psum"])
        act_chain, dve_chain, pool_chain = map(sem, ["act_chain", "dve_chain", "pool_chain"])
        (z_psum, z_hi, z_lo, q_copied, k_copied, abs_done, softplus_ready, b_ready,
         v_copied, r_silu, r_scaled, d_ready, e_ready, qk_ready, s_psum, s_taken, reset_set,
         khat_ready, khat_psum, khat_copied, qhat_ready, kv_psum, state_ready, o_psum, ms_ready,
         o_rstd_ready, o_ready, oT_psum, oT_hi, oT_lo) = map(sem, [
             "z_psum", "z_hi", "z_lo", "q_copied", "k_copied", "abs_done", "softplus_ready",
             "b_ready", "v_copied", "r_silu", "r_scaled", "d_ready", "e_ready",
             "qk_ready", "s_psum", "s_taken", "reset_set", "khat_ready", "khat_psum", "khat_copied",
             "qhat_ready", "kv_psum", "state_ready", "o_psum", "ms_ready", "o_rstd_ready", "o_ready",
             "oT_psum", "oT_hi", "oT_lo"])
        (lam_exp, c_ready, conv_init, xc_taken, conv_ready, xc_hi_ready, xc_lo_ready, gelu_ready,
         r_psum, r_ready, i_ready, la_ready, a_ready, th_ready, a2_ready, m2_ready, m_ready, ix_ready,
         h_ready, y_ready, y_hi, y_lo) = map(sem, [
             "lam_exp", "c_ready", "conv_init", "xc_taken", "conv_ready", "xc_hi_ready", "xc_lo_ready",
             "gelu_ready", "r_psum", "r_ready", "i_ready", "la_ready", "a_ready", "th_ready", "a2_ready",
             "m2_ready", "m_ready", "ix_ready", "h_ready", "y_ready", "y_hi", "y_lo"])
        (gate_tile_done, gate_ready, sig_ready) = map(sem, ["gate_tile_done", "gate_ready", "sig_ready"])
        first_psum, first_copied, first_turned = map(sem, ["first_psum", "first_copied", "first_turned"])
        unit_landed = [sem(f"unit_landed{u}") for u in range(UNITS)]
        xT_landed = [sem(f"xT_landed{u}") for u in range(UNITS)]
        first_hi, first_lo, xT_second_landed, first_x_hi, first_x_lo, warm_ready = map(
            sem, ["first_hi", "first_lo", "xT_second_landed", "first_x_hi", "first_x_lo", "warm_ready"])

        KINDS = ["ffn", "gla", "ffn", "ple", "ffn", "lru", "ffn", "ple"][:phases]
        n_pieces = BASES[phases] if phases < len(SIZES) else PIECES
        FFN_OF = {0: 0, 2: 1, 4: 2, 6: 3}
        LN_OF = {0: 0, 1: 1, 2: 2, 4: 3, 5: 4, 6: 5}
        PLE_OF = {3: 0, 7: 1}
        FIRST_OF = {2: 0, 4: 1, 5: 2, 6: 3}

        def f32(ap):
            return ap.bitcast(F32)

        def tok(t):
            return slice(t * P, (t + 1) * P)

        def half(h):
            return slice(h * HALF, (h + 1) * HALF)

        def unit_of(K, q):
            if K != LT:
                return divmod(q, K)
            return q // UNITS % 2, q // (2 * UNITS) * UNITS + q % UNITS

        block = ctx.enter_context(nc.Block())

        @block.sync
        def _(sp):
            for u in range(UNITS):
                sp.dma_start(xT_in[:, u], xT_d[:, u]).then_inc(xT_landed[u], 16)
                sp.dma_start(raw[:, 0, u], stream[0][:, u * HALF:(u + 1) * HALF]).then_inc(unit_landed[u], 16)
            sp.dma_start(xT_in[:, HT:], xT_d[:, HT:]).then_inc(xT_second_landed, 16)
            for n in range(1, RING):
                sp.dma_start(raw[:, n].rearrange("p u n -> p (u n)"), stream[n]).then_inc(raw_landed[n], 16)
            sp.wait_ge(first_lo, UNITS - 1)
            full = n_pieces // RING
            with sp.Fori(1, full) as i:
                for s in range(RING):
                    sp.wait_ge(lo_ready, RING * i + (s - RING + 1))
                    sp.dma_start(raw[:, s].rearrange("p u n -> p (u n)"),
                                 stream[bass.ds(RING * i + s, 1), :, :].rearrange("a p n -> p (a n)")
                                 ).then_inc(raw_landed[s], 16)
            for n in range(full * RING, n_pieces):
                sp.wait_ge(lo_ready, n - RING + 1)
                sp.dma_start(raw[:, n % RING].rearrange("p u n -> p (u n)"), stream[n]
                             ).then_inc(raw_landed[n % RING], 16)
            for t in range(TT):
                sp.wait_ge(x_half_ready, 4 * (phases - 1) + 2 * (t + 1))
                sp.dma_start(out[tok(t), :], x_rows[:, t]).then_inc(out_landed, 16)
            sp.wait_ge(out_landed, 16 * TT)

        @block.tensor
        def _(pe):
            def piece_ready(n):
                pe.wait_ge(lo_ready, n + 1)

            def x_ready(i, t, h):
                pe.wait_ge(xT_lo_ready, 4 * i + 2 * t + h + 1)

            def feature_units(slot, k0, units, bank, x_hi, x_lo, first, last):
                for u in units:
                    k = k0 + u - units[0]
                    for m in range(HT):
                        o = ps[:, bank + m // 2, (m % 2) * T:(m % 2 + 1) * T]
                        wh, wl = (w[:, slot, u, m * P:(m + 1) * P] for w in (w_hi, w_lo))
                        pe.matmul(o, wh, x_hi[:, k], start=first and u == 0 and m % 2 == 0,
                                  stop=False, skip_group_check=True)
                        pe.matmul(o, wh, x_lo[:, k], start=False, stop=False, skip_group_check=True)
                        mm = pe.matmul(o, wl, x_hi[:, k], start=False, stop=last and u == UNITS - 1,
                                       skip_group_check=True)
                return mm

            def row_unit(slot, u, bank, k, t, x_hi, x_lo, first, last):
                o = ps[:, bank, :]
                xh, xl = x_hi[:, k, tok(t)], x_lo[:, k, tok(t)]
                pe.matmul(o, xh, w_hi[:, slot, u, :], start=first, stop=False)
                pe.matmul(o, xh, w_lo[:, slot, u, :], start=False, stop=False)
                return pe.matmul(o, xl, w_hi[:, slot, u, :], start=False, stop=last)

            def feature_chunk(n, bank, x_hi=xT_hi, x_lo=xT_lo):
                for j in range(2):
                    piece_ready(n + j)
                    mm = feature_units((n + j) % RING, UNITS * j, range(UNITS), bank, x_hi, x_lo, j == 0, j == 1)
                    mm.then_inc(piece_used, 1)

            def turn_x(i, t, h):
                pe.wait_ge(x_half_ready, 4 * i + 2 * t + h + 1)
                for j in range(HT):
                    mm = pe.transpose(ps[:, 2 * t + h, tok(j)],
                                      x_rows[:, t, h * HALF + j * P:h * HALF + (j + 1) * P], ident)
                mm.then_inc(xT_psum, 1)

            def turn_o(t):
                pe.wait_ge(o_ready, HEADS * (t + 1))
                for h in range(2):
                    for j in range(HT):
                        mm = pe.transpose(ps[:, 4 - 4 * t + h, tok(j)],
                                          o_rows[:, t, h * HALF + j * P:h * HALF + (j + 1) * P], ident)
                    mm.then_inc(oT_psum, 1)

            def first_tiles(i, n, bank, tile_0_done):
                for t in range(TT):
                    if t == 0:
                        turn_x(i - 1, 0, 1)
                    for j in range(2):
                        x_ready(i, t, j)
                        piece_ready(n + j)
                        for u in range(UNITS):
                            if t == 0 and j == 1 and u == 3:
                                turn_x(i - 1, 1, 0)
                            mm = row_unit((n + j) % RING, u, bank + t, UNITS * j + u, t, xT_hi, xT_lo,
                                          j == 0 and u == 0, j == 1 and u == UNITS - 1)
                        if t == 1:
                            mm.then_inc(piece_used, 1)
                    if t == 0 and tile_0_done is not None:
                        mm.then_inc(tile_0_done, 1)
                    if t == 0:
                        turn_x(i - 1, 1, 1)

            def first_chunk(i, n):
                if i == 0:
                    for j in range(2):
                        if j == 1:
                            pe.wait_ge(xT_lo_ready, 4)
                        for u in range(UNITS):
                            if j == 0:
                                pe.wait_ge(first_x_lo, u + 1)
                            if j == 0 and u < UNITS - 1:
                                pe.wait_ge(first_lo, u + 1)
                            else:
                                piece_ready(n + j)
                            mm = feature_units(j, UNITS * j + u, [u], 0, xT_hi, xT_lo, j == 0, j == 1)
                        mm.then_inc(piece_used, 1)
                    return
                first_tiles(i, n, 4, first_psum)
                for t in range(TT):
                    pe.wait_ge(first_copied, 2 * FIRST_OF[i] + t + 1)
                    for m in range(HT):
                        mm = pe.transpose(ps[:, m // 2, (m % 2) * T + t * P:(m % 2) * T + (t + 1) * P],
                                          first_rows[:, t, m * P:(m + 1) * P], ident)
                mm.then_inc(first_turned, 1)

            def out_proj(i, n0, K, wait_k):
                units = 2 * K
                late = units - 2 * UNITS
                if K == KD:
                    turn_o(0)
                    for t in range(TT):
                        for q in range(late):
                            n = n0 + q // UNITS
                            if t == 0 and q == late - 2:
                                turn_o(1)
                            if q % HT == 0:
                                piece_ready(n)
                                pe.wait_ge(oT_lo, 2 * t + q // HT + 1)
                            mm = row_unit(n % RING, q % UNITS, 4 + t, q, t, hT_hi, hT_lo, q == 0, q == K - 1)
                            if t == 1 and q % UNITS == UNITS - 1:
                                mm.then_inc(piece_used, 1)
                for q in range(late if K != KD else 0):
                    h, k = unit_of(K, q)
                    n = n0 + q // UNITS
                    if q % UNITS == 0:
                        piece_ready(n)
                    if h == 0:
                        wait_k(k)
                    for t in range(TT):
                        mm = row_unit(n % RING, q % UNITS, 4 + 2 * h + t, k, t, hT_hi, hT_lo, k == 0, k == K - 1)
                    if q % UNITS == UNITS - 1:
                        mm.then_inc(piece_used, 1)
                    elif q == K - 1 and K != LT:
                        mm.then_inc(half_done, 1)
                for t in range(TT):
                    for q in range(late, units):
                        h, k = unit_of(K, q)
                        n = n0 + q // UNITS
                        if q % UNITS == 0:
                            piece_ready(n)
                            wait_k(k)
                        if t == 1 and q == units - 2 and i + 1 < len(KINDS):
                            turn_x(i, 0, 0)
                        mm = row_unit(n % RING, q % UNITS, 4 + 2 * h + t, k, t, hT_hi, hT_lo, k == 0, k == K - 1)
                        if t == 1 and q % UNITS == UNITS - 1:
                            mm.then_inc(piece_used, 1)
                        elif t == 0 and (q == units - 1 or K == LT and q % UNITS == UNITS - 1):
                            mm.then_inc(tile_done, 1)

            def ffn(i):
                f, n = FFN_OF[i], BASES[i]
                first_chunk(i, n)

                with pe.Fori(0, (CHUNKS - 1) // 2) as it:
                    for j in range(2):
                        pe.wait_ge(hidden_ready, 2 * it + (CHUNKS * f + j))
                        for jj in range(2):
                            m = 2 + 2 * j + jj
                            pe.wait_ge(lo_ready, 4 * it + (n + m + 1))
                            mm = feature_units((n + m) % RING, UNITS * jj, range(UNITS), 2 * ((1 + j) % 2), xT_hi,
                                               xT_lo, jj == 0, jj == 1)
                            mm.then_inc(piece_used, 1)

                def wait_k(k):
                    if k == 0:
                        pe.wait_ge(hidden_lo, CHUNKS * f + CHUNKS - 1)
                    if k == KF - 2:
                        pe.wait_ge(hidden_lo, CHUNKS * f + CHUNKS)

                if i == 0:
                    pe.wait_ge(params_landed, 16)
                out_proj(i, n + FFN_IN, KF, wait_k)

            def ple(i):
                l, n = PLE_OF[i], BASES[i]
                first_tiles(i, n, 4, gate_tile_done)
                piece_ready(n + 2)
                pe.wait_ge(pT_lo_ready, l + 1)
                for c, banks in ((0, (6, 7)), (1, (1, 3))):
                    for t in range(TT):
                        for k in range(2):
                            mm = row_unit((n + 2) % RING, 2 * c + k, banks[t], k, t, pT_hi, pT_lo, k == 0, k == 1)
                mm.then_inc(piece_used, 1)
                for t in range(TT):
                    for j in range(2):
                        piece_ready(n + 3 + j)
                        for u in range(UNITS):
                            if t == 1 and j == 1 and u == 2 and i + 1 < len(KINDS):
                                turn_x(i, 0, 0)
                            mm = row_unit((n + 3 + j) % RING, u, 2 * t, UNITS * j + u, t, xT_hi, xT_lo,
                                          j == 0 and u == 0, j == 1 and u == UNITS - 1)
                        if t == 1:
                            mm.then_inc(piece_used, 1)
                    if t == 0:
                        mm.then_inc(gate_tile_done, 1)

            def gla(i):
                n, ln = BASES[i], LN_OF[i]
                first_tiles(i, n, 6, None)
                slot = (n + 2) % RING

                def gate_logits():
                    pe.wait_ge(z_lo, 1)
                    pe.wait_ge(v_copied, 1)
                    for h in range(HEADS):
                        o = ps[:, 5 + h // 2, (h % 2) * T:(h % 2 + 1) * T]
                        wh, wl = (w[:, slot, 2, h * P:(h + 1) * P] for w in (w_hi, w_lo))
                        pe.matmul(o, wh, zT_hi[:], start=h % 2 == 0, stop=False, skip_group_check=True)
                        pe.matmul(o, wh, zT_lo[:], start=False, stop=False, skip_group_check=True)
                        mm = pe.matmul(o, wl, zT_hi[:], start=False, stop=True, skip_group_check=True)
                    mm.then_inc(piece_used, 2)

                piece_ready(n + 2)
                for k in range(KD):
                    o = ps[:, 4, 0:T]
                    wh, wl = (w[:, slot, k // HT, (k % HT) * P:(k % HT + 1) * P] for w in (w_hi, w_lo))
                    pe.matmul(o, wh, xT_hi[:, k], start=k == 0, stop=False)
                    pe.matmul(o, wh, xT_lo[:, k], start=False, stop=False)
                    mm = pe.matmul(o, wl, xT_hi[:, k], start=False, stop=k == KD - 1)
                mm.then_inc(z_psum, 1)
                for j in range(2):
                    piece_ready(n + 3 + j)
                    mm = feature_units((n + 3 + j) % RING, UNITS * j, range(UNITS), 2, xT_hi, xT_lo, j == 0, j == 1)
                    if j == 0:
                        gate_logits()
                mm.then_inc(piece_used, 1)
                feature_chunk(n + 5, 0)

                def rows_piece(m, bank):
                    j = (m - 7) % 2
                    piece_ready(n + m)
                    for u in range(UNITS):
                        for t in range(TT):
                            mm = row_unit((n + m) % RING, u, bank + t, UNITS * j + u, t, xT_hi, xT_lo,
                                          j == 0 and u == 0, j == 1 and u == UNITS - 1)
                    mm.then_inc(piece_used, 1)

                def level(l):
                    bank = 4 + 2 * (l % 2)
                    if l < LEVELS:
                        pe.wait_ge(qk_ready, 2 * (l + 1))
                    if l == 0:
                        pe.wait_ge(b_ready, 1)
                    if l >= 2:
                        pe.wait_ge(s_taken, l - 1)
                    for g in range(2 * HEADS):
                        a, b = (qk[l % 2], qk[l % 2]) if l < LEVELS else (kT, qT)
                        mm = pe.matmul(ps[:, bank + g // 4, (g % 4) * P:(g % 4 + 1) * P], a[:, g * P:(g + 1) * P],
                                       b[:, g * P:(g + 1) * P], start=True, stop=True, skip_group_check=True)
                    mm.then_inc(s_psum, 1)

                pe.wait_ge(q_copied, 1)
                rows_piece(7, 2)
                rows_piece(8, 2)
                level(0)
                pe.wait_ge(k_copied, 1)
                rows_piece(9, 0)
                level(1)
                rows_piece(10, 0)
                level(2)
                pe.wait_ge(v_copied, 2)
                rows_piece(11, 2)
                level(3)
                rows_piece(12, 2)
                level(4)
                level(5)
                pe.wait_ge(khat_ready, 1)
                pe.wait_ge(r_silu, 1)
                for g in range(2 * HEADS):
                    mm = pe.transpose(ps[:, g // 4, (g % 4) * P:(g % 4 + 1) * P], qk[0][:, g * P:(g + 1) * P], ident)
                mm.then_inc(khat_psum, 1)
                level(6)
                pe.wait_ge(khat_copied, 1)
                for c, bank in enumerate([2, 0, 4]):
                    if c == 0:
                        pe.wait_ge(r_silu, 2)
                    if c == 2:
                        pe.wait_ge(s_taken, LEVELS + 1)
                    rows = slice(LC * (c % 2), LC * (c % 2) + LC)
                    for h in range(HEADS):
                        mm = pe.matmul(ps[:, bank + h // 2, (h % 2) * DV:(h % 2 + 1) * DV],
                                       khat_rows[rows, 2 * h + c // 2, :],
                                       v_rows[rows, c // 2, h * DV:(h + 1) * DV],
                                       start=True, stop=True, skip_group_check=True)
                    mm.then_inc(kv_psum, 1)
                pe.wait_ge(s_taken, LEVELS + 1)
                for t, bank in ((0, 6), (1, 2)):
                    if t == 0:
                        pe.wait_ge(qhat_ready, 1)
                        pe.wait_ge(state_ready, 1)
                    for h in range(HEADS):
                        pe.matmul(ps[:, bank + h // 2, (h % 2) * DV:(h % 2 + 1) * DV], scores[:, 2 * h + t, :],
                                  v_rows[:, t, h * DV:(h + 1) * DV], start=h % 2 == 0, stop=False, skip_group_check=True)
                    pe.wait_ge(state_ready, 1 + 2 * HEADS * t)
                    for h in range(HEADS):
                        for c in (2 * t, 2 * t + 1):
                            if c > 0:
                                oc = ps[LC * (c % 2):LC * (c % 2) + LC, bank + h // 2, (h % 2) * DV:(h % 2 + 1) * DV]
                                mm = pe.matmul(oc, qhat[:, h * T + c * LC:h * T + (c + 1) * LC], state[c - 1][:, h, :],
                                               start=False, stop=True, skip_group_check=True)
                    mm.then_inc(o_psum, 1)

                out_proj(i, n + 13, KD, lambda k: None)

            def lru(i):
                n, ln = BASES[i], LN_OF[i]

                def gates(g):
                    m = n + GATES_AT[g]
                    piece_ready(m)
                    pe.wait_ge(xc_lo_ready, g + 1)
                    if g:
                        pe.wait_ge(i_ready, 4 * g)
                    slot = m % RING
                    for gate in range(2):
                        for b in range(2):
                            for k in range(2):
                                for mt in range(2):
                                    o = ps[:, 4 + 2 * gate + b, mt * T:(mt + 1) * T]
                                    wh, wl = (w[:, slot, 2 * b + gate, k * T + mt * P:k * T + (mt + 1) * P]
                                              for w in (w_hi, w_lo))
                                    pe.matmul(o, wh, xc_hi[:, 2 * b + k], start=k == 0 and mt == 0, stop=False,
                                              skip_group_check=True)
                                    pe.matmul(o, wh, xc_lo[:, 2 * b + k], start=False, stop=False,
                                              skip_group_check=True)
                                    mm = pe.matmul(o, wl, xc_hi[:, 2 * b + k], start=False, stop=k == 1,
                                                   skip_group_check=True)
                        mm.then_inc(piece_used if gate else r_psum, 1)

                first_chunk(i, n + CONV_AT[0])
                for g in range(LRU_GROUPS):
                    if g:
                        pe.wait_ge(gelu_ready, g)
                    feature_chunk(n + GELU_AT[g], 2)
                    if g + 1 < LRU_GROUPS:
                        pe.wait_ge(conv_ready, CONV_STEPS * (g + 1))
                        feature_chunk(n + CONV_AT[g + 1], 0)
                    gates(g)

                def wait_k(k):
                    if k == 0:
                        pe.wait_ge(i_ready, LT)
                    if k % 4 == 0:
                        pe.wait_ge(y_lo, k // 4 + 1)

                out_proj(i, n + 5 * LRU_GROUPS, LT, wait_k)

            for i, kind in enumerate(KINDS):
                {"ffn": ffn, "gla": gla, "lru": lru, "ple": ple}[kind](i)

        @block.scalar
        def _(act):
            issued = [1]
            links = [0]

            def split_one(slot, landed, free):
                act.wait_ge(raw_landed[slot], landed)
                if free is not None:
                    act.wait_ge(piece_used, free)
                act.activation(w_hi[:, slot], raw[:, slot], ACT.Copy).then_inc(hi_ready, 1)

            def split_to(m):
                while issued[0] <= min(m, n_pieces - 1):
                    n = issued[0]
                    split_one(n % RING, 16 * (n // RING + (n % RING > 0)), n - RING + 1 if n >= RING else None)
                    issued[0] += 1

            def chain(ins):
                links[0] += 1
                ins.then_inc(act_chain, 1)
                act.wait_ge(act_chain, links[0])

            def x_high(i, t):
                if i + 1 < len(KINDS):
                    for h in range(2):
                        act.wait_ge(xT_psum, 4 * i + 2 * t + h + 1)
                        act.activation(xT_hi[:, HT * h:HT * (h + 1), tok(t)],
                                       ps[:, 2 * t + h, :].rearrange("p (j n) -> p j n", n=P), ACT.Copy
                                       ).then_inc(xT_hi_ready, 1)

            def out_split(i, n0, K):
                last = n0 + 2 * K // UNITS - 1
                split_to(last + 3)
                x_high(i, 0)
                x_high(i, 1)

            def first_copy(i, n, between):
                if i:
                    act.wait_ge(first_psum, FIRST_OF[i] + 1)
                    act.activation(first_rows[:, 0], ps[:, 4, :], ACT.Copy).then_inc(first_copied, 1)
                    between()
                    act.wait_ge(piece_used, n + 2)
                    act.activation(first_rows[:, 1], ps[:, 5, :], ACT.Copy).then_inc(first_copied, 1)

            def ffn(i):
                f, n = FFN_OF[i], BASES[i]

                def chunk(par, before, after, c, silu_free):
                    before()
                    if i and silu_free is None:
                        act.wait_ge(first_turned, FIRST_OF[i] + 1)
                    else:
                        act.wait_ge(piece_used, 2 * c + (n + 2))
                    if silu_free is not None:
                        act.wait_ge(hidden_ready, silu_free)
                    act.activation(silu_t[:, par], ps[:, 2 * par, :], ACT.Silu).then_inc(silu_done, 1)
                    after()
                    act.wait_ge(hidden_ready, c + (CHUNKS * f + 1))
                    act.activation(hT_hi[:, bass.ds(2 * c, 2), :],
                                   hid_t[:, par].rearrange("p (k t) -> p k t", t=T), ACT.Copy).then_inc(hidden_hi, 1)

                split_to(n + 2)
                first_copy(i, n, lambda: split_to(n + 3))
                if f:
                    load_p(f)
                chunk(0, lambda: split_to(n + 3), lambda: split_to(n + 4), 0, None)
                with act.Fori(0, (CHUNKS - 1) // 2) as it:
                    for j in range(2):
                        def split(m):
                            split_one((n + m) % RING, 16 * it + 16 * ((n + m) // RING + ((n + m) % RING > 0)), 4 * it + (n + m - 3))
                        chunk((1 + j) % 2, lambda: split(5 + 2 * j), lambda: split(6 + 2 * j), 2 * it + (1 + j),
                              2 * it + (CHUNKS * f + j))
                issued[0] += 4 * ((CHUNKS - 1) // 2)
                if i == 0:
                    act.wait_ge(params_landed, 16)
                    chain(act.activation(small[:, 0], small_in[:, C_LAM:C_LAM + LT], ACT.Abs))
                    act.activation(small[:, 0], small[:, 0], ACT.Exp, scale=-1.0).then_inc(lam_exp, 1)
                out_split(i, n + FFN_IN, KF)

            def load_p(f):
                if f in (1, 3):
                    act.wait_ge(pT_landed, 16 * (f // 2 + 1))
                    if f == 3:
                        act.wait_ge(piece_used, BASES[3] + 3)
                    act.activation(pT_hi[:], pT[:], ACT.Copy).then_inc(pT_hi_ready, 1)

            def ple(i):
                l, n = PLE_OF[i], BASES[i]
                split_to(n + 3)
                for c in range(2):
                    for t in range(TT):
                        act.wait_ge(gate_ready, 4 * l + 2 * c + t + 1)
                        act.activation(ple_gate[:, c, t], ple_gate[:, c, t], ACT.Sigmoid).then_inc(sig_ready, 1)
                        if c == 0:
                            split_to(n + 4 + 2 * t)
                        elif t == 0:
                            x_high(i, 0)
                x_high(i, 1)

            def gla(i):
                n, ln = BASES[i], LN_OF[i]
                S = lambda m: split_to(n + m)

                def v_copy(c, bank):
                    act.wait_ge(piece_used, n + 2 + 7 * c)
                    act.activation(v_rows[:, :, half(c)], ps[:, bank:bank + 2, :], ACT.Copy).then_inc(v_copied, 1)

                S(3)
                v_copy(0, 6)
                S(4)
                act.wait_ge(z_psum, 1)
                act.activation(zT_hi[:], ps[:, 4, 0:T], ACT.Copy).then_inc(z_hi, 1)
                S(5)
                S(6)
                act.wait_ge(piece_used, n + 4)
                for h in range(HEADS):
                    act.activation(dec[0][:, h * T:(h + 1) * T], ps[:, 5 + h // 2, (h % 2) * T:(h % 2 + 1) * T], ACT.Abs,
                                   bias=small_in[:, C_BGATE + h:C_BGATE + h + 1]).then_inc(abs_done, 1)
                act.wait_ge(abs_done, HEADS)
                chain(act.activation(dec[0][:], dec[0][:], ACT.Exp, scale=-1.0))
                act.activation(dec[0][:], dec[0][:], ACT.Ln, bias=1.0).then_inc(softplus_ready, 1)
                S(7)
                act.wait_ge(piece_used, n + 5)
                act.activation(qT[:], ps[:, 2:4, :].rearrange("p a b -> p (a b)"), ACT.Copy,
                               scale=float(P) ** -0.5).then_inc(q_copied, 1)
                S(8)
                S(9)
                act.wait_ge(piece_used, n + 7)
                act.activation(kT[:], ps[:, 0:2, :].rearrange("p a b -> p (a b)"), ACT.Copy).then_inc(k_copied, 1)
                S(10)

                def decay_of(l):
                    act.wait_ge(d_ready, 2 * (l + 1))
                    act.activation(dec[l % 2][:], dec[l % 2][:], ACT.Exp, scale=1.0 / TAU).then_inc(e_ready, 1)

                def r_gate(c):
                    act.wait_ge(piece_used, n + 11 + 2 * c)
                    act.activation(r_rows[:, :, half(c)], ps[:, 2 * c:2 * c + 2, :], ACT.Silu).then_inc(r_silu, 1)

                decay_of(0)
                decay_of(1)
                S(11)
                v_copy(1, 2)
                decay_of(2)
                S(12)
                decay_of(3)
                S(13)
                decay_of(4)
                S(14)
                r_gate(0)
                decay_of(5)
                act.wait_ge(qk_ready, 2 * 5)
                act.activation(dec[0][:], bcum[:], ACT.Exp, scale=1.0 / TAU).then_inc(e_ready, 1)
                S(15)
                act.wait_ge(d_ready, 2 * LEVELS + 1)
                act.activation(dec[1][:], dec[1][:], ACT.Exp, scale=1.0 / TAU).then_inc(e_ready, 1)
                r_gate(1)
                S(16)
                act.wait_ge(khat_psum, 1)
                act.wait_ge(s_psum, LEVELS)
                act.activation(khat_rows[:].rearrange("p a b -> p (a b)"), ps[:, 0:2, :].rearrange("p a b -> p (a b)"),
                               ACT.Copy).then_inc(khat_copied, 1)
                act.wait_ge(kv_psum, 1)
                act.activation(state[0][:].rearrange("p a b -> p (a b)"), ps[:, 2:4, :].rearrange("p a b -> p (a b)"),
                               ACT.Copy).then_inc(state_ready, 1)
                for t, bank in ((0, 6), (1, 2)):
                    act.wait_ge(o_psum, t + 1)
                    if t:
                        act.wait_ge(ms_ready, HEADS)
                    for h in range(HEADS):
                        act.activation(squares[:, h], ps[:, bank + h // 2, (h % 2) * DV:(h % 2 + 1) * DV], ACT.Square,
                                       accum_out=o_ms[:, t, h:h + 1]).then_inc(ms_ready, 1)
                for t, bank in ((0, 4), (1, 0)):
                    for h in range(2):
                        act.wait_ge(oT_psum, 2 * t + h + 1)
                        act.activation(hT_hi[:, HT * h:HT * (h + 1), tok(t)],
                                       ps[:, bank + h, :].rearrange("p (j n) -> p j n", n=P), ACT.Copy).then_inc(oT_hi, 1)
                out_split(i, n + 13, KD)

            def lru(i):
                n, ln = BASES[i], LN_OF[i]
                S = lambda m: split_to(n + m)

                def conv_first(g):
                    if g == 0:
                        act.wait_ge(first_turned, FIRST_OF[i] + 1)
                    else:
                        act.wait_ge(piece_used, n + CONV_AT[g] + 2)
                    if g >= 2:
                        act.wait_ge(xc_taken, g - 1)
                    for j in range(4):
                        ch = 4 * g + j
                        w = C_CONVW + ch * CONV + CONV - 1
                        act.activation(xc_T[g % 2][:, j], ps[:, j // 2, (j % 2) * T:(j % 2 + 1) * T], ACT.Identity,
                                       scale=small_in[:, w:w + 1], bias=small_in[:, C_CONVB + ch:C_CONVB + ch + 1]
                                       ).then_inc(conv_init, 1)

                def xc_high(g):
                    act.wait_ge(conv_ready, CONV_STEPS * (g + 1))
                    if g:
                        act.wait_ge(piece_used, n + GATES_AT[g - 1] + 1)
                    act.activation(xc_hi[:], xc_T[g % 2][:], ACT.Copy).then_inc(xc_hi_ready, 1)

                def gelu(g):
                    act.wait_ge(piece_used, n + GELU_AT[g] + 2)
                    if g:
                        act.wait_ge(y_ready, g)
                    act.activation(gelu_T[:].rearrange("p a b -> p (a b)"), ps[:, 2:4, :].rearrange("p a b -> p (a b)"),
                                   ACT.Gelu_apprx_tanh).then_inc(gelu_ready, 1)

                def sigmoids(g):
                    if g >= 2:
                        act.wait_ge(y_hi, g - 1)
                        act.wait_ge(y_lo, g - 1)
                    for gate, dst, done, bias in ((0, r_T[g % 2], r_ready, C_BA), (1, i_T[g % 2], i_ready, C_BI)):
                        if gate == 0:
                            act.wait_ge(r_psum, g + 1)
                        else:
                            act.wait_ge(piece_used, n + GATES_AT[g] + 1)
                        for j in range(4):
                            act.activation(dst[:, j], ps[:, 4 + 2 * gate + j // 2, (j % 2) * T:(j % 2 + 1) * T], ACT.Sigmoid,
                                           bias=small_in[:, bias + 4 * g + j:bias + 4 * g + j + 1]).then_inc(done, 1)

                def exp_tanh(g):
                    act.wait_ge(la_ready, 4 * (g + 1))
                    act.activation(a_T[:], r_T[g % 2][:], ACT.Exp).then_inc(a_ready, 1)
                    act.activation(m_T[:], r_T[g % 2][:], ACT.Tanh, scale=-1.0).then_inc(th_ready, 1)

                def root(g):
                    act.wait_ge(m2_ready, g + 1)
                    act.activation(m_T[:], m_T[:], ACT.Sqrt).then_inc(m_ready, 1)

                def y_high(g):
                    act.wait_ge(y_ready, g + 1)
                    act.activation(hT_hi[:, 4 * g:4 * (g + 1)], i_T[g % 2][:], ACT.Copy).then_inc(y_hi, 1)

                S(2)
                first_copy(i, n, lambda: S(3))
                conv_first(0)
                S(5)
                xc_high(0)
                S(6)
                gelu(0)
                S(8)
                conv_first(1)
                S(9)
                sigmoids(0)
                for g in range(LRU_GROUPS - 1):
                    m = 5 * g
                    xc_high(g + 1)
                    exp_tanh(g)
                    S(m + 10)
                    if g + 2 < LRU_GROUPS:
                        S(m + 11)
                        root(g)
                        S(m + 12)
                        y_high(g)
                        gelu(g + 1)
                        S(m + 13)
                        conv_first(g + 2)
                        S(m + 14)
                        sigmoids(g + 1)
                    else:
                        S(m + 11)
                        sigmoids(g + 1)
                        root(g)
                        S(m + 13)
                        y_high(g)
                g = LRU_GROUPS - 1
                exp_tanh(g)
                S(19)
                root(g)
                gelu(g)
                S(20)
                y_high(g)
                out_split(i, n + 5 * LRU_GROUPS, LT)

            act.wait_ge(warm_ready, 1)
            act.activation(small[:, 4], small[:, 5], ACT.Copy).then_inc(act_chain, 1)
            links[0] += 1
            for u in range(UNITS):
                act.wait_ge(xT_landed[u], 16)
                act.activation(xT_hi[:, u], xT_in[:, u], ACT.Copy).then_inc(first_x_hi, 1)
                act.wait_ge(unit_landed[u], 16)
                act.activation(w_hi[:, 0, u], raw[:, 0, u], ACT.Copy
                               ).then_inc(first_hi if u < UNITS - 1 else hi_ready, 1)
            act.wait_ge(xT_second_landed, 16)
            act.activation(xT_hi[:, HT:], xT_in[:, HT:], ACT.Copy).then_inc(xT_hi_ready, 4)
            split_to(2)
            for i, kind in enumerate(KINDS):
                {"ffn": ffn, "gla": gla, "lru": lru, "ple": ple}[kind](i)

        @block.vector
        def _(dve):
            issued = [1]
            links = [0]

            def split_one(slot, ready):
                dve.wait_ge(hi_ready, ready)
                dve.tensor_tensor(w_lo[:, slot], raw[:, slot], f32(w_hi[:, slot]), ALU.subtract).then_inc(lo_ready, 1)

            def split_to(m):
                while issued[0] <= min(m, n_pieces - 1):
                    split_one(issued[0] % RING, issued[0] + 1)
                    issued[0] += 1

            def chain(ins):
                links[0] += 1
                ins.then_inc(dve_chain, 1)
                dve.wait_ge(dve_chain, links[0])

            def add_residual(t, h, coef):
                chain(dve.scalar_tensor_tensor(out=u_rows[:, t, half(h)], in0=ps[:, 4 + 2 * h + t, :], scalar=coef,
                                               in1=x_rows[:, t, half(h)], op0=ALU.mult, op1=ALU.add))
                chain(dve.bn_stats(stats[:, t, h], u_rows[:, t, half(h)]))

            def x_low(i, t):
                for h in range(2 if i + 1 < len(KINDS) else 0):
                    dve.wait_ge(xT_hi_ready, 4 * (i + 1) + 2 * t + h + 1)
                    dst = (slice(None), slice(HT * h, HT * (h + 1)), tok(t))
                    dve.tensor_tensor(xT_lo[dst], ps[:, 2 * t + h, :].rearrange("p (j n) -> p j n", n=P),
                                      f32(xT_hi[dst]), ALU.subtract).then_inc(xT_lo_ready, 1)

            def out_norm(i, n0, K, coef):
                ln = LN_OF[i]
                last = n0 + 2 * K // UNITS - 1
                split_to(n0 + (K - 1) // UNITS + 3)
                if K == LT:
                    pass
                elif K % UNITS:
                    dve.wait_ge(half_done, ln // 3 * 2 + (ln % 3) // 2 + 1)
                else:
                    dve.wait_ge(piece_used, n0 + K // UNITS)
                if K != LT:
                    for t in range(TT):
                        add_residual(t, 0, coef)
                split_to(last + (1 if K == LT else 2))
                dve.wait_ge(row_params_landed, 16 * (i + 1))
                for t in range(TT):
                    if K == LT:
                        if t == 0:
                            dve.wait_ge(tile_done, ln + 1)
                        else:
                            split_to(last + 2)
                            dve.wait_ge(piece_used, last)
                        add_residual(t, 0, coef)
                    if t == 0:
                        dve.wait_ge(tile_done, ln + 1 + (i >= 5))
                    else:
                        dve.wait_ge(piece_used, last + 1)
                    add_residual(t, 1, coef)
                    dve.bn_aggr(mean_var[:, t], stats[:, t].rearrange("p a b -> p (a b)")).then_inc(stats_ready, 1)
                    dve.wait_ge(stats_ready, 2 * ln + t + 1)
                    for h in range(2):
                        chain(dve.scalar_tensor_tensor(out=u_rows[:, t, half(h)], in0=u_rows[:, t, half(h)],
                                                       scalar=mean_var[:, t, 0:1], in1=row_params[:, 0, half(h)],
                                                       op0=ALU.subtract, op1=ALU.mult))
                        if h == 0:
                            dve.wait_ge(rstd_ready, 2 * ln + t + 1)
                        dve.scalar_tensor_tensor(out=x_rows[:, t, half(h)], in0=u_rows[:, t, half(h)],
                                                 scalar=rstd[:, t, 1:2], in1=row_params[:, 1, half(h)],
                                                 op0=ALU.mult, op1=ALU.add).then_inc(x_half_ready, 1)
                    if t == 0:
                        x_low(i, 0)
                x_low(i, 1)
                split_to(last + 3)

            def constants():
                u, s, s2, poly, neg = (small[:, j] for j in range(5))
                dve.wait_ge(lam_exp, 1)
                chain(dve.tensor_scalar(s, u, 2.0, None, ALU.add))
                chain(dve.reciprocal(s, s))
                chain(dve.tensor_tensor(s, s, u, ALU.mult))
                chain(dve.tensor_tensor(s2, s, s, ALU.mult))
                chain(dve.tensor_scalar(poly, s2, 1.0 / 19, 1.0 / 17, ALU.mult, ALU.add))
                for odd in range(15, 0, -2):
                    chain(dve.tensor_tensor(poly, poly, s2, ALU.mult))
                    chain(dve.tensor_scalar(poly, poly, 1.0 / odd, None, ALU.add))
                chain(dve.tensor_tensor(poly, poly, s, ALU.mult))
                chain(dve.tensor_scalar(neg, small_in[:, C_LAM:C_LAM + LT], -1.0, 0.0, ALU.mult, ALU.max))
                chain(dve.scalar_tensor_tensor(out=poly, in0=poly, scalar=2.0, in1=neg, op0=ALU.mult, op1=ALU.add))
                dve.tensor_scalar(lru_c[:], poly, -LRU_C, None, ALU.mult).then_inc(c_ready, 1)
                dve.wait_ge(masks_landed, 16)
                dve.tensor_copy(mask[:], mask_in[:]).then_inc(masks_ready, 1)

            def ffn(i):
                f, n = FFN_OF[i], BASES[i]

                def chunk(par, before, after, c, hid_free):
                    before()
                    dve.wait_ge(silu_done, c + (CHUNKS * f + 1))
                    if hid_free is not None:
                        dve.wait_ge(hidden_hi, hid_free)
                    dve.tensor_tensor(hid_t[:, par], silu_t[:, par], ps[:, 2 * par + 1, :], ALU.mult
                                      ).then_inc(hidden_ready, 1)
                    after()
                    dve.wait_ge(hidden_hi, c + (CHUNKS * f + 1))
                    dst = hT_lo[:, bass.ds(2 * c, 2), :]
                    dve.tensor_tensor(dst, hid_t[:, par].rearrange("p (k t) -> p k t", t=T),
                                      f32(hT_hi[:, bass.ds(2 * c, 2), :]), ALU.subtract).then_inc(hidden_lo, 1)

                split_to(n + 2)
                if f in (1, 3):
                    dve.wait_ge(pT_hi_ready, f // 2 + 1)
                    dve.tensor_tensor(pT_lo[:], pT[:], f32(pT_hi[:]), ALU.subtract).then_inc(pT_lo_ready, 1)
                chunk(0, lambda: split_to(n + 3), lambda: split_to(n + 4), 0, None)
                with dve.Fori(0, (CHUNKS - 1) // 2) as it:
                    for j in range(2):
                        def split(m):
                            split_one((n + m) % RING, 4 * it + (n + m + 1))
                        chunk((1 + j) % 2, lambda: split(5 + 2 * j), lambda: split(6 + 2 * j), 2 * it + (1 + j),
                              2 * it + (CHUNKS * f + j))
                issued[0] += 4 * ((CHUNKS - 1) // 2)
                if i == 0:
                    constants()
                    dve.wait_ge(x_landed, 16)
                out_norm(i, n + FFN_IN, KF, 0.5 / ALPHA)

            def ple(i):
                l, n = PLE_OF[i], BASES[i]
                split_to(n + 3)
                dve.wait_ge(row_params_landed, 16 * (i + 1))

                def biased(c, t):
                    if t == 0:
                        dve.wait_ge(gate_tile_done, 2 * l + c + 1)
                    else:
                        dve.wait_ge(piece_used, n + 2 + 3 * c)
                    dve.tensor_tensor(ple_gate[:, c, t], ps[:, 2 * t if c else 4 + t, :], row_params[:, 0, half(c)], ALU.add
                                      ).then_inc(gate_ready, 1)

                def add(c, t):
                    dve.wait_ge(sig_ready, 4 * l + 2 * c + t + 1)
                    chain(dve.tensor_tensor(ple_gate[:, c, t], ple_gate[:, c, t], ps[:, 2 * t + 1 if c else 6 + t, :], ALU.mult))
                    return dve.tensor_tensor(x_rows[:, t, half(c)], x_rows[:, t, half(c)], ple_gate[:, c, t], ALU.add)

                biased(0, 0)
                split_to(n + 4)
                biased(0, 1)
                dve.wait_ge(piece_used, n + 3)
                chain(add(0, 0))
                chain(add(0, 1))
                split_to(n + 5)
                biased(1, 0)
                add(1, 0).then_inc(x_half_ready, 2)
                biased(1, 1)
                x_low(i, 0)
                add(1, 1).then_inc(x_half_ready, 2)
                split_to(n + 6)
                x_low(i, 1)

            def gla(i):
                n, ln = BASES[i], LN_OF[i]
                S = lambda m: split_to(n + m)
                S(4)
                dve.wait_ge(z_hi, 1)
                dve.tensor_tensor(zT_lo[:], ps[:, 4, 0:T], f32(zT_hi[:]), ALU.subtract).then_inc(z_lo, 1)
                S(6)
                dve.wait_ge(abs_done, HEADS)
                for h in range(HEADS):
                    last = dve.tensor_scalar(dec[1][:, h * T:(h + 1) * T], ps[:, 5 + h // 2, (h % 2) * T:(h % 2 + 1) * T],
                                             small_in[:, C_BGATE + h:C_BGATE + h + 1], 0.0, ALU.add, ALU.min)
                    if h < HEADS - 1:
                        last.then_inc(dve_chain, 1)
                links[0] += HEADS - 1
                chain(last)
                S(7)
                dve.wait_ge(softplus_ready, 1)
                chain(dve.tensor_tensor(dec[1][:], dec[1][:], dec[0][:], ALU.subtract))
                dve.wait_ge(reset_set, 2)
                dve.tensor_tensor_scan(bcum[:], qk[0][:], dec[1][:], 0.0, ALU.mult, ALU.add).then_inc(b_ready, 1)
                S(9)

                def operands(l):
                    size = LC >> l
                    dve.wait_ge(e_ready, l + 1)
                    if l == 0:
                        dve.wait_ge(q_copied, 1)
                        dve.wait_ge(k_copied, 1)
                        dve.wait_ge(b_ready, 1)
                    if l >= 2:
                        dve.wait_ge(s_psum, l - 1)
                    for src, part in ((kT, slice(0, size // 2)), (qT, slice(size // 2, size))):
                        blocks = [a[:].rearrange("p (b s) -> p b s", s=size)[:, :, part] for a in (qk[l % 2], dec[l % 2], src)]
                        dve.tensor_tensor(*blocks, ALU.mult).then_inc(qk_ready, 1)

                def take(l):
                    dve.wait_ge(s_psum, l + 1)
                    bank = 4 + 2 * (l % 2)
                    dve.copy_predicated(scores[:], mask[:, l:l + 1, :].to_broadcast([P, 2 * HEADS, P]),
                                        ps[:, bank:bank + 2, :].rearrange("p a (b n) -> p (a b) n", n=P)
                                        ).then_inc(s_taken, 1)
                    dve.wait_ge(s_taken, l + 1)

                operands(0)
                S(10)
                for l in range(LEVELS + 1):
                    if l + 1 < LEVELS:
                        operands(l + 1)
                    if l == LEVELS - 1:
                        dve.wait_ge(e_ready, LEVELS + 2)
                        dve.wait_ge(s_psum, LEVELS - 1)
                        dve.tensor_tensor(qk[0][:], dec[1][:], kT[:], ALU.mult).then_inc(khat_ready, 1)
                        dve.tensor_copy(decay[:], dec[0][:].rearrange("p (b s) -> p b s", s=LC)[:, :, LC - 1]
                                        ).then_inc(dve_chain, 1)
                        links[0] += 1
                    S(min(11 + l, 15))
                    if l == 0:
                        dve.wait_ge(reset_set, 3)
                        dve.wait_ge(masks_ready, 1)
                    if l == LEVELS:
                        dve.wait_ge(piece_used, n + 13)
                        dve.tensor_tensor(qhat[:], dec[0][:], qT[:], ALU.mult).then_inc(qhat_ready, 1)
                    take(l)
                S(16)
                dve.wait_ge(dve_chain, links[0])
                dve.wait_ge(state_ready, 1)
                for c in (1, 2):
                    bank = 4 * (c - 1)
                    dve.wait_ge(kv_psum, c + 1)
                    for h in range(HEADS):
                        dve.scalar_tensor_tensor(out=state[c][:, h], in0=state[c - 1][:, h],
                                                 scalar=decay[:, h * 4 + c:h * 4 + c + 1],
                                                 in1=ps[:, bank + h // 2, (h % 2) * DV:(h % 2 + 1) * DV],
                                                 op0=ALU.mult, op1=ALU.add).then_inc(state_ready, 1)
                    if c == 1:
                        dve.wait_ge(state_ready, 1 + HEADS)
                dve.wait_ge(r_scaled, 1)
                for t, bank in ((0, 6), (1, 2)):
                    dve.wait_ge(o_rstd_ready, t + 1)
                    for h in range(HEADS):
                        dve.scalar_tensor_tensor(out=o_rows[:, t, h * DV:(h + 1) * DV],
                                                 in0=ps[:, bank + h // 2, (h % 2) * DV:(h % 2 + 1) * DV],
                                                 scalar=o_rstd[:, t, h:h + 1], in1=r_rows[:, t, h * DV:(h + 1) * DV],
                                                 op0=ALU.mult, op1=ALU.mult).then_inc(o_ready, 1)
                    for h in range(2):
                        dve.wait_ge(oT_hi, 2 * t + h + 1)
                        dst = (slice(None), slice(HT * h, HT * (h + 1)), tok(t))
                        dve.tensor_tensor(hT_lo[dst], ps[:, 4 - 4 * t + h, :].rearrange("p (j n) -> p j n", n=P),
                                          f32(hT_hi[dst]), ALU.subtract).then_inc(oT_lo, 1)
                out_norm(i, n + 13, KD, 1.0 / ALPHA)

            def lru(i):
                n, ln = BASES[i], LN_OF[i]
                S = lambda m: split_to(n + m)

                def taps(g):
                    dve.wait_ge(conv_init, 4 * (g + 1))
                    xc = xc_T[g % 2]
                    for back in range(1, CONV):
                        for j in range(4):
                            w = C_CONVW + (4 * g + j) * CONV + CONV - 1 - back
                            dve.scalar_tensor_tensor(out=xc[:, j, back:], in0=ps[:, j // 2, (j % 2) * T:(j % 2 + 1) * T - back],
                                                     scalar=small_in[:, w:w + 1], in1=xc[:, j, back:],
                                                     op0=ALU.mult, op1=ALU.add).then_inc(conv_ready, 1)
                        if back < CONV - 1:
                            dve.wait_ge(conv_ready, CONV_STEPS * g + HT * back)

                def xc_low(g):
                    dve.wait_ge(xc_hi_ready, g + 1)
                    dve.tensor_tensor(xc_lo[:], xc_T[g % 2][:], f32(xc_hi[:]), ALU.subtract).then_inc(xc_lo_ready, 1)

                def log_a(g):
                    dve.wait_ge(r_ready, 4 * (g + 1))
                    if g == 0:
                        dve.wait_ge(c_ready, 1)
                    for j in range(4):
                        dve.tensor_scalar(r_T[g % 2][:, j], r_T[g % 2][:, j], lru_c[:, 4 * g + j:4 * g + j + 1], None, ALU.mult
                                          ).then_inc(la_ready, 1)

                def keep(g):
                    dve.wait_ge(th_ready, g + 1)
                    dve.wait_ge(a2_ready, g + 1)
                    chain(dve.scalar_tensor_tensor(out=m_T[:], in0=r_T[g % 2][:], scalar=1.0, in1=m_T[:],
                                                   op0=ALU.add, op1=ALU.mult))
                    dve.tensor_scalar(m_T[:], m_T[:], 0.0, None, ALU.max).then_inc(m2_ready, 1)

                def recurrence(g):
                    dve.wait_ge(m_ready, g + 1)
                    dve.wait_ge(xc_taken, g + 1)
                    dve.tensor_tensor(i_T[g % 2][:], i_T[g % 2][:], m_T[:], ALU.mult).then_inc(ix_ready, 1)
                    dve.wait_ge(ix_ready, g + 1)
                    for j in range(4):
                        dve.tensor_tensor_scan(r_T[g % 2][:, j], a_T[:, j], i_T[g % 2][:, j], 0.0, ALU.mult, ALU.add).then_inc(h_ready, 1)
                    dve.wait_ge(h_ready, 4 * (g + 1))
                    dve.wait_ge(gelu_ready, g + 1)
                    dve.tensor_tensor(i_T[g % 2][:], r_T[g % 2][:], gelu_T[:], ALU.mult).then_inc(y_ready, 1)

                def y_low(g):
                    dve.wait_ge(y_hi, g + 1)
                    dve.tensor_tensor(hT_lo[:, 4 * g:4 * (g + 1)], i_T[g % 2][:], f32(hT_hi[:, 4 * g:4 * (g + 1)]), ALU.subtract
                                      ).then_inc(y_lo, 1)

                S(3)
                taps(0)
                S(5)
                xc_low(0)
                S(8)
                taps(1)
                S(9)
                log_a(0)
                for g in range(LRU_GROUPS - 1):
                    m = 5 * g
                    xc_low(g + 1)
                    S(m + 10)
                    keep(g)
                    if g + 2 < LRU_GROUPS:
                        S(m + 11)
                        recurrence(g)
                        S(m + 12)
                        y_low(g)
                        S(m + 13)
                        taps(g + 2)
                        S(m + 14)
                        log_a(g + 1)
                    else:
                        S(m + 11)
                        recurrence(g)
                        log_a(g + 1)
                        y_low(g)
                        S(m + 13)
                g = LRU_GROUPS - 1
                keep(g)
                S(19)
                recurrence(g)
                y_low(g)
                out_norm(i, n + 5 * LRU_GROUPS, LT, 1.0 / ALPHA)

            dve.memset(small[:, 5], 0.0).then_inc(warm_ready, 1)
            for u in range(UNITS):
                dve.wait_ge(first_x_hi, u + 1)
                dve.tensor_tensor(xT_lo[:, u], xT_in[:, u], f32(xT_hi[:, u]), ALU.subtract).then_inc(first_x_lo, 1)
                if u < UNITS - 1:
                    dve.wait_ge(first_hi, u + 1)
                else:
                    dve.wait_ge(hi_ready, 1)
                dve.tensor_tensor(w_lo[:, 0, u], raw[:, 0, u], f32(w_hi[:, 0, u]), ALU.subtract
                                  ).then_inc(first_lo if u < UNITS - 1 else lo_ready, 1)
            dve.wait_ge(xT_hi_ready, 4)
            dve.tensor_tensor(xT_lo[:, HT:], xT_in[:, HT:], f32(xT_hi[:, HT:]), ALU.subtract).then_inc(xT_lo_ready, 4)
            split_to(3)
            for i, kind in enumerate(KINDS):
                {"ffn": ffn, "gla": gla, "lru": lru, "ple": ple}[kind](i)

        @block.gpsimd
        def _(pool):
            links = [0]

            def chain(ins):
                links[0] += 1
                ins.then_inc(pool_chain, 1)
                pool.wait_ge(pool_chain, links[0])

            def load_rows(i):
                if i < len(KINDS):
                    if i:
                        pool.wait_ge(x_half_ready, 4 * i)
                    pool.dma_start(row_params[:].rearrange("p a b -> p (a b)"), row_params_d[i].partition_broadcast(P)
                                   ).then_inc(row_params_landed, 16)

            def inverse_root(dst, src, scale, eps):
                width = dst.shape[-1]
                chain(pool.tensor_scalar(dst, src, scale, eps, ALU.mult, ALU.add))
                return pool.tensor_tensor(dst, dst, expo[:, 0:width], ALU.pow)

            def norm(i):
                ln = LN_OF[i]
                for t in range(TT):
                    pool.wait_ge(stats_ready, 2 * ln + t + 1)
                    inverse_root(rstd[:, t, 1:2], mean_var[:, t, 1:2], 1.0, EPS / ALPHA ** 2).then_inc(rstd_ready, 1)
                load_rows(i + 1)

            def gla(i):
                pool.wait_ge(piece_used, BASES[1])
                pool.memset(qk[0][:], 1.0).then_inc(reset_set, 1)
                pool.wait_ge(reset_set, 1)
                pool.memset(qk[0][:].rearrange("p (b s) -> p b s", s=LC)[:, :, 0:1], 0.0).then_inc(reset_set, 1)
                pool.memset(scores[:], 0.0).then_inc(reset_set, 1)
                pool.wait_ge(b_ready, 1)
                for l in range(LEVELS):
                    size = LC >> l
                    bb = bcum[:].rearrange("p (b s) -> p b s", s=size)
                    dd = dec[l % 2][:].rearrange("p (b s) -> p b s", s=size)
                    mid = bb[:, :, size // 2 - 1:size // 2].to_broadcast([P, HEADS * T // size, size // 2])
                    if l >= 2:
                        pool.wait_ge(qk_ready, 2 * (l - 1))
                    pool.tensor_tensor(dd[:, :, 0:size // 2], mid, bb[:, :, 0:size // 2], ALU.subtract).then_inc(d_ready, 1)
                    pool.tensor_tensor(dd[:, :, size // 2:size], bb[:, :, size // 2:size], mid, ALU.subtract
                                       ).then_inc(d_ready, 1)
                bb = bcum[:].rearrange("p (b s) -> p b s", s=LC)
                pool.wait_ge(qk_ready, 2 * LEVELS)
                pool.tensor_tensor(dec[1][:].rearrange("p (b s) -> p b s", s=LC),
                                   bb[:, :, LC - 1:LC].to_broadcast([P, HEADS * T // LC, LC]), bb, ALU.subtract
                                   ).then_inc(d_ready, 1)
                pool.wait_ge(r_silu, 2)
                rr = r_rows[:].rearrange("p t (h v) -> p (t h) v", v=DV)
                pool.tensor_tensor(rr, rr, small_in[:, C_NORMG:C_NORMG + DV].unsqueeze(1).to_broadcast([P, TT * HEADS, DV]),
                                   ALU.mult).then_inc(r_scaled, 1)
                for t in range(TT):
                    pool.wait_ge(ms_ready, HEADS * (t + 1))
                    inverse_root(o_rstd[:, t], o_ms[:, t], 1.0 / DV, EPS).then_inc(o_rstd_ready, 1)
                norm(i)

            def lru(i):
                for g in range(LRU_GROUPS):
                    pool.wait_ge(i_ready, 4 * (g + 1))
                    pool.tensor_tensor(i_T[g % 2][:], i_T[g % 2][:], xc_T[g % 2][:], ALU.mult).then_inc(xc_taken, 1)
                    pool.wait_ge(a_ready, g + 1)
                    pool.wait_ge(th_ready, g + 1)
                    pool.tensor_tensor(r_T[g % 2][:], a_T[:], a_T[:], ALU.mult).then_inc(a2_ready, 1)
                norm(i)

            def ple(i):
                if PLE_OF[i] == 0:
                    pool.wait_ge(pT_lo_ready, 1)
                    pool.dma_start(pT[:], pT_d[1]).then_inc(pT_landed, 16)
                load_rows(i + 1)

            pool.wait_ge(raw_landed[RING - 1], 16)
            pool.dma_start(small_in[:], params_d).then_inc(params_landed, 16)
            pool.dma_start(mask_in[:], masks_d).then_inc(masks_landed, 16)
            pool.dma_start(x_rows[:], x_rows_d).then_inc(x_landed, 16)
            pool.dma_start(pT[:], pT_d[0]).then_inc(pT_landed, 16)
            load_rows(0)
            chain(pool.memset(expo[:], -0.5))
            for i, kind in enumerate(KINDS):
                {"ffn": norm, "gla": gla, "lru": lru, "ple": ple}[kind](i)


def level_masks():
    s, t = np.meshgrid(np.arange(P), np.arange(P), indexing="ij")
    out = []
    for l in range(LEVELS):
        size = LC >> l
        out.append((s // size == t // size) & (s % size < size // 2) & (t % size >= size // 2))
    out.append(s == t)
    return np.stack(out, 1).astype(np.float32)


def pack(x, p, ln_g, ln_b, ffn_w_in, ffn_w_out, gla_w_in, gla_w_gate_up, gla_b_gate, gla_norm_g, gla_w_out,
         lru_w_in, lru_conv_w, lru_conv_b, lru_w_a, lru_b_a, lru_w_i, lru_b_i, lru_lambda, lru_w_out,
         ple_w_gate, ple_b_gate, ple_w_proj):
    zero = np.zeros((P, HALF), np.float32)

    def chunks(w):
        return [w[k * P:(k + 1) * P, c * HALF:(c + 1) * HALF]
                for c in range(w.shape[1] // HALF) for k in range(w.shape[0] // P)]

    def ffn(layer, which):
        w = ffn_w_in[layer, which]
        q = HALF // 2
        paired = np.concatenate([w[:, o + q * c:o + q * (c + 1)] for c in range(CHUNKS) for o in (0, F)], 1)
        return chunks(paired) + chunks(ffn_w_out[layer, which])

    def gla():
        w = gla_w_in[0]
        kw = HEADS * P
        cuts = [0, kw, 2 * kw, 2 * kw + D, 2 * kw + 2 * D]
        wz = w[:, cuts[4]:]
        z = np.zeros((KD, P, P), np.float32)
        z[:, :, :wz.shape[1]] = wz.reshape(KD, P, -1)
        z = z.transpose(1, 0, 2).reshape(P, KD * P)
        up = zero.copy()
        up[:wz.shape[1]] = gla_w_gate_up[0]
        parts = [w[:, a:b] for a, b in zip(cuts, cuts[1:])]
        q, k, v, r = map(chunks, parts)
        return v[:KD] + [z[:, :HALF], z[:, HALF:], up, zero] + q + k + v[KD:] + r + chunks(gla_w_out[0])

    def lru():
        w = lru_w_in[0]
        width = w.shape[1] // 2
        units = []
        at = {}
        for g in range(LRU_GROUPS):
            cols = slice(g * HALF, (g + 1) * HALF)
            at[CONV_AT[g]] = chunks(w[:, :width][:, cols])
            at[GELU_AT[g]] = chunks(w[:, width:][:, cols])
            at[GATES_AT[g]] = [np.concatenate([m[0, b, :P], m[0, b, P:]], 1)
                               for b in (2 * g, 2 * g + 1) for m in (lru_w_a, lru_w_i)]
        for m in sorted(at):
            units += at[m]
        o = chunks(lru_w_out[0])
        return units + [o[h * LT + g * UNITS + k] for g in range(LRU_GROUPS) for h in range(2) for k in range(UNITS)]

    def ple(layer):
        gate, proj = chunks(ple_w_gate[layer]), chunks(ple_w_proj[layer])
        return gate[:KD] + proj + gate[KD:]

    units = ffn(0, 0) + gla() + ffn(0, 1) + ple(0) + ffn(1, 0) + lru() + ffn(1, 1) + ple(1)
    stream = np.empty((PIECES, P, UNITS, HALF), np.float32)
    for q, unit in enumerate(units):
        stream[q // UNITS, :, q % UNITS] = unit
    assert len(units) == PIECES * UNITS

    def column(v):
        return np.asarray(v).reshape(-1, P).T

    small = np.concatenate([
        column(gla_b_gate[0]), np.broadcast_to(gla_norm_g[0], (P, DV)),
        lru_conv_w[0].T.reshape(LT, P, CONV).transpose(1, 0, 2).reshape(P, LT * CONV), column(lru_conv_b[0]),
        column(lru_b_a[0]), column(lru_b_i[0]), column(lru_lambda[0]), np.eye(P, dtype=np.float32)], 1)
    norms = iter(range(6))
    by_phase = [np.concatenate([ple_b_gate[i // 4]] * 2) if i % 4 == 3 else
                  (lambda m: np.concatenate([ln_g[m // 3, m % 3], ln_b[m // 3, m % 3]]))(next(norms))
                  for i in range(len(SIZES))]
    return {
        "stream": stream.reshape(PIECES, P, UNITS * HALF),
        "x_rows": x[0].reshape(TT, P, D).transpose(1, 0, 2),
        "xT": x[0].T.reshape(KD, P, T).transpose(1, 0, 2),
        "pT": p[:, 0].transpose(0, 2, 1).reshape(2, 2, P, T).transpose(0, 2, 1, 3),
        "row_params": np.stack(by_phase),
        "params": small,
        "masks": level_masks(),
    }


def kernel(**inputs):
    import concourse.bacc as bacc
    from concourse.bass_utils import run_bass_kernel_spmd

    arrays = {k: np.ascontiguousarray(v) for k, v in pack(**{k: np.asarray(v) for k, v in inputs.items()}).items()}
    nc = bacc.Bacc("TRN2", target_bir_lowering=False, num_devices=1)
    args = [nc.dram_tensor(k, v.shape, mybir.dt.from_np(v.dtype), kind="ExternalInput").ap() for k, v in arrays.items()]
    out = nc.dram_tensor("out", [T, D], F32, kind="ExternalOutput").ap()
    build(nc, *args, out)
    r = run_bass_kernel_spmd(nc, [arrays], core_ids=[0])
    return r.results[0]["out"].reshape(1, T, D)
```
